# Optimizing a Trainium2 kernel written in Bass

```python
import jax, jax.numpy as jnp
from jax import lax
import numpy as np

D_MODEL = 1024
BATCH = 1
SEQ = 256
DEPTH = 2

GRID_W = 64
CTX_LEN = 256
EPS = 1e-6
D_FF = 2816
LRU_WIDTH = 512
LRU_HEADS = 8
LRU_HEAD_DIM = LRU_WIDTH // LRU_HEADS
CONV_WIDTH = 4
CONV_LEFT = 2
RG_C = 8.0
MLP_GROUPS = 4
MLP_GROUP_DIM = 128
MLP_WIDTH = MLP_GROUPS * MLP_GROUP_DIM
CHUNK = 128
ROWS_PER_CHUNK = CHUNK // GRID_W
MIX_WIDTH = LRU_WIDTH + MLP_WIDTH
IN_PROJ_WIDTH = 2 * LRU_WIDTH + 2 * MLP_WIDTH
N_MOD = 9

kernel_name = "hybrid_rglru_chunkmlp_macaron_dit"

def rmsnorm(x, g):
    x32 = x.astype(jnp.float32)
    y = x32 * lax.rsqrt(jnp.mean(x32 * x32, axis=-1, keepdims=True) + EPS)
    return (y * g.astype(jnp.float32)).astype(x.dtype)

def layernorm(x, g):
    x32 = x.astype(jnp.float32)
    mu = jnp.mean(x32, axis=-1, keepdims=True)
    xc = x32 - mu
    y = xc * lax.rsqrt(jnp.mean(xc * xc, axis=-1, keepdims=True) + EPS)
    return (y * g.astype(jnp.float32)).astype(x.dtype)

def modulate(z, shift, scale):
    return z * (1.0 + scale) + shift

def swiglu(z, w_in, w_out):
    gate, up = jnp.split(z @ w_in, 2, axis=-1)
    return (jax.nn.silu(gate) * up) @ w_out

def short_conv(x, w, b):
    n = x.shape[1]
    xp = jnp.pad(x, ((0, 0), (CONV_LEFT, CONV_WIDTH - 1 - CONV_LEFT), (0, 0)))
    y = b
    for k in range(CONV_WIDTH):
        y = y + xp[:, k:k + n] * w[k]
    return y

def rglru_coeffs(xc, w_r, b_r, w_i, b_i, lam):
    bsz, n, _ = xc.shape
    xh = xc.reshape(bsz, n, LRU_HEADS, LRU_HEAD_DIM)
    r = jax.nn.sigmoid(jnp.einsum("bnhd,hde->bnhe", xh, w_r).reshape(bsz, n, LRU_WIDTH) + b_r)
    i = jax.nn.sigmoid(jnp.einsum("bnhd,hde->bnhe", xh, w_i).reshape(bsz, n, LRU_WIDTH) + b_i)
    log_a = (-RG_C * r * jax.nn.softplus(-lam)).astype(jnp.float32)
    a = jnp.exp(log_a)
    b = jnp.sqrt(-jnp.expm1(2.0 * log_a)) * (i * xc).astype(jnp.float32)
    return a, b

def _combine(left, right):
    a_l, b_l = left
    a_r, b_r = right
    return a_l * a_r, a_r * b_l + b_r

def linear_scan(a, b, h0, reverse):
    a_cum, h = lax.associative_scan(_combine, (a, b), reverse=reverse, axis=1)
    return h + a_cum * h0[:, None, :]

def lru_scans(xl, conv_w, conv_b, w_r, b_r, w_i, b_i, lam, h0_f, h0_b):
    xc = short_conv(xl, conv_w, conv_b)
    a_f, b_f = rglru_coeffs(xc, w_r[0], b_r[0], w_i[0], b_i[0], lam[0])
    h_f = linear_scan(a_f, b_f, h0_f, reverse=False)
    a_b, b_b = rglru_coeffs(xc, w_r[1], b_r[1], w_i[1], b_i[1], lam[1])
    h_b = linear_scan(a_b, b_b, h0_b, reverse=True)
    return h_f, h_b

def spatial_gating(u, v, norm_g, w_s, b_s, n_chunks):
    bsz = v.shape[0]
    v = layernorm(v, norm_g)
    vc = v.reshape(bsz, n_chunks, CHUNK, MLP_GROUPS, MLP_GROUP_DIM)
    z = jnp.einsum("gpq,bnqgc->bnpgc", w_s, vc) + b_s.T[None, None, :, :, None]
    return u * z.reshape(u.shape)

def mix_out(p, h_f, h_b, sgu_norm_g, sgu_w, sgu_b, w_out, n_chunks):
    gl = p[..., LRU_WIDTH:2 * LRU_WIDTH]
    u = p[..., 2 * LRU_WIDTH:2 * LRU_WIDTH + MLP_WIDTH]
    v = p[..., 2 * LRU_WIDTH + MLP_WIDTH:]
    y_lru = (h_f + h_b).astype(p.dtype) * jax.nn.gelu(gl)
    y_sgu = spatial_gating(u, v, sgu_norm_g, sgu_w, sgu_b, n_chunks)
    return jnp.concatenate([y_lru, y_sgu], axis=-1) @ w_out

def setup_inputs(seed: int = 0) -> dict:
    key = jax.random.key(seed)
    ks = jax.random.split(key, 32)
    f32 = jnp.float32

    def nrm(k, shape, s):
        return jax.random.normal(k, shape, f32) * s

    def gain(k, shape):
        return 1.0 + 0.02 * jax.random.normal(k, shape, f32)

    u = jax.random.uniform(ks[20], (DEPTH, 2, LRU_WIDTH), f32, minval=0.9, maxval=0.999)
    a0 = u ** (1.0 / RG_C)
    lru_lambda = jnp.log(a0) - jnp.log1p(-a0)

    return {
        "x": nrm(ks[0], (BATCH, SEQ, D_MODEL), 1.0),
        "c": nrm(ks[1], (BATCH, D_MODEL), 1.0),
        "ctx": nrm(ks[2], (BATCH, CTX_LEN, D_MODEL), 1.0),
        "c_ctx": nrm(ks[3], (D_MODEL,), 1.0),
        "w_ada": nrm(ks[4], (DEPTH, D_MODEL, N_MOD * D_MODEL), 0.5 * D_MODEL ** -0.5),
        "b_ada": nrm(ks[5], (DEPTH, N_MOD * D_MODEL), 0.02),
        "ffn1_norm_g": gain(ks[6], (DEPTH, D_MODEL)),
        "ffn1_w_in": nrm(ks[7], (DEPTH, D_MODEL, 2 * D_FF), D_MODEL ** -0.5),
        "ffn1_w_out": nrm(ks[8], (DEPTH, D_FF, D_MODEL), D_FF ** -0.5),
        "mix_norm_g": gain(ks[9], (DEPTH, D_MODEL)),
        "w_in_mix": nrm(ks[10], (DEPTH, D_MODEL, IN_PROJ_WIDTH), D_MODEL ** -0.5),
        "lru_conv_w": nrm(ks[11], (DEPTH, CONV_WIDTH, LRU_WIDTH), CONV_WIDTH ** -0.5),
        "lru_conv_b": nrm(ks[12], (DEPTH, LRU_WIDTH), 0.02),
        "lru_w_r": nrm(ks[13], (DEPTH, 2, LRU_HEADS, LRU_HEAD_DIM, LRU_HEAD_DIM), LRU_HEAD_DIM ** -0.5),
        "lru_b_r": nrm(ks[14], (DEPTH, 2, LRU_WIDTH), 0.02),
        "lru_w_i": nrm(ks[15], (DEPTH, 2, LRU_HEADS, LRU_HEAD_DIM, LRU_HEAD_DIM), LRU_HEAD_DIM ** -0.5),
        "lru_b_i": nrm(ks[16], (DEPTH, 2, LRU_WIDTH), 0.02),
        "lru_lambda": lru_lambda,
        "sgu_norm_g": gain(ks[17], (DEPTH, MLP_WIDTH)),
        "sgu_w": nrm(ks[18], (DEPTH, MLP_GROUPS, CHUNK, CHUNK), CHUNK ** -0.5),
        "sgu_b": nrm(ks[19], (DEPTH, MLP_GROUPS, CHUNK), 0.02),
        "w_out_mix": nrm(ks[21], (DEPTH, MIX_WIDTH, D_MODEL), MIX_WIDTH ** -0.5),
        "ffn2_norm_g": gain(ks[22], (DEPTH, D_MODEL)),
        "ffn2_w_in": nrm(ks[23], (DEPTH, D_MODEL, 2 * D_FF), D_MODEL ** -0.5),
        "ffn2_w_out": nrm(ks[24], (DEPTH, D_FF, D_MODEL), D_FF ** -0.5),
        "final_norm_g": gain(ks[25], (D_MODEL,)),
    }

def reference(x, c, ctx, c_ctx, w_ada, b_ada, ffn1_norm_g, ffn1_w_in, ffn1_w_out,
              mix_norm_g, w_in_mix, lru_conv_w, lru_conv_b, lru_w_r, lru_b_r, lru_w_i,
              lru_b_i, lru_lambda, sgu_norm_g, sgu_w, sgu_b, w_out_mix,
              ffn2_norm_g, ffn2_w_in, ffn2_w_out, final_norm_g):
    bsz, n_lat, _ = x.shape
    rows = n_lat // GRID_W
    n_chunks_lat = rows // ROWS_PER_CHUNK
    n_chunks_ctx = CTX_LEN // CHUNK
    zeros_state = jnp.zeros((bsz, LRU_WIDTH), jnp.float32)

    sc = jax.nn.silu(c)
    scc = jax.nn.silu(c_ctx)[None, :]
    h, hc = x, ctx
    for l in range(DEPTH):
        last = l == DEPTH - 1
        m = jnp.split((sc @ w_ada[l] + b_ada[l])[:, None, :], N_MOD, axis=-1)
        mc = jnp.split((scc @ w_ada[l] + b_ada[l])[:, None, :], N_MOD, axis=-1)

        h = h + 0.5 * m[2] * swiglu(modulate(rmsnorm(h, ffn1_norm_g[l]), m[0], m[1]),
                                    ffn1_w_in[l], ffn1_w_out[l])
        hc = hc + 0.5 * mc[2] * swiglu(modulate(rmsnorm(hc, ffn1_norm_g[l]), mc[0], mc[1]),
                                       ffn1_w_in[l], ffn1_w_out[l])

        lru_p = (lru_conv_w[l], lru_conv_b[l], lru_w_r[l], lru_b_r[l],
                 lru_w_i[l], lru_b_i[l], lru_lambda[l])
        zc = modulate(rmsnorm(hc, mix_norm_g[l]), mc[3], mc[4])
        if not last:
            pc = zc @ w_in_mix[l]
            hf_c, hb_c = lru_scans(pc[..., :LRU_WIDTH], *lru_p, zeros_state, zeros_state)
            hc = hc + mc[5] * mix_out(pc, hf_c, hb_c, sgu_norm_g[l], sgu_w[l], sgu_b[l],
                                      w_out_mix[l], n_chunks_ctx)
        else:
            hf_c, hb_c = lru_scans(zc @ w_in_mix[l][:, :LRU_WIDTH], *lru_p,
                                   zeros_state, zeros_state)
        z = modulate(rmsnorm(h, mix_norm_g[l]), m[3], m[4])
        p = z @ w_in_mix[l]
        hf, hb = lru_scans(p[..., :LRU_WIDTH], *lru_p, hf_c[:, -1], hb_c[:, 0])
        h = h + m[5] * mix_out(p, hf, hb, sgu_norm_g[l], sgu_w[l], sgu_b[l],
                               w_out_mix[l], n_chunks_lat)

        h = h + 0.5 * m[8] * swiglu(modulate(rmsnorm(h, ffn2_norm_g[l]), m[6], m[7]),
                                    ffn2_w_in[l], ffn2_w_out[l])
        if not last:
            hc = hc + 0.5 * mc[8] * swiglu(modulate(rmsnorm(hc, ffn2_norm_g[l]), mc[6], mc[7]),
                                           ffn2_w_in[l], ffn2_w_out[l])

    return rmsnorm(h, final_norm_g)


_drawn_inputs = setup_inputs


def setup_inputs(seed=0):
    import zlib

    import numpy as np

    out = dict(_drawn_inputs(seed))
    spreads = {}
    factors = {'ffn1_norm_g': 8.0,
     'mix_norm_g': 3.915,
     'lru_b_r': 37.353,
     'lru_b_i': 32.555,
     'sgu_norm_g': 8.0,
     'sgu_b': 8.0,
     'ffn2_norm_g': 8.0,
     'final_norm_g': 7.949,
     'lru_conv_b': 3.174}
    for name, (base, spread) in spreads.items():
        noise = np.random.default_rng([zlib.crc32(name.encode()), seed]).standard_normal(out[name].shape)
        drawn = base * np.exp(spread * noise) if base else spread * noise
        out[name] = __import__('jax').numpy.asarray(drawn.astype(out[name].dtype))
    for name, factor in factors.items():
        out[name] = (out[name] * factor).astype(out[name].dtype)
    return out
```

```python
from contextlib import ExitStack

import numpy as np
import concourse.bass as bass
from concourse import mybir

F32 = mybir.dt.float32
F32R = mybir.dt.float32r
ACT = mybir.ActivationFunctionType
ALU = mybir.AluOpType
AX_X = mybir.AxisListType.X

P = 128
D = 1024
KD = D // P
SEQ = 256
T = 512
DFF = 2816
KF = DFF // P
DEPTH = 2
LT = 4
NMOD = 9
EPS = 1e-6

RING = 4
SLOT = 8 * P
UP_SLOTS = 2 * KF
DOWN_SLOTS = 24
IN_SLOTS = 16
OUT_SLOTS = 8
LAYER_SLOTS = 2 * (UP_SLOTS + DOWN_SLOTS) + IN_SLOTS + OUT_SLOTS
SLOTS = DEPTH * LAYER_SLOTS

CHUNKS = DEPTH * NMOD * 2
LAYER_CHUNKS = NMOD * 2
UNITS = 4 * CHUNKS
ADA_RING = 2
HEAD_CHUNKS = 4
UP_ADA = {(0, 0): 11, (0, 1): 11, (1, 0): 4, (1, 1): 0}
DOWN_ADA = {(0, 0): 6, (0, 1): 0, (1, 0): 0, (1, 1): 0}

C_CVEC = 0
C_BADA = C_CVEC + KD * 2
C_GAIN = C_BADA + DEPTH * NMOD * KD
C_CONV = C_GAIN + (DEPTH * 3 + 1) * KD
C_BR = C_CONV + DEPTH * 5 * LT
C_BI = C_BR + DEPTH * 2 * LT
C_LAM = C_BI + DEPTH * 2 * LT
C_SGU = C_LAM + DEPTH * 2 * LT
N_PAR = C_SGU + DEPTH * LT


def schedule():
    at, slot, chunk, ffn, tile = {}, 0, HEAD_CHUNKS, 0, 0
    for l in range(DEPTH):
        for part in ("ffn0", "mix", "ffn1"):
            if part == "mix":
                at[l, "in"] = dict(slot=slot, chunk=chunk)
                slot += IN_SLOTS
                at[l, "out"] = dict(slot=slot, tile=tile)
                slot += OUT_SLOTS
            else:
                f = int(part[3])
                at[l, "up", f] = dict(slot=slot, chunk=chunk, ffn=ffn, ada=UP_ADA[l, f])
                slot += UP_SLOTS
                chunk += UP_ADA[l, f]
                at[l, "down", f] = dict(slot=slot, chunk=chunk, ffn=ffn, tile=tile, ada=DOWN_ADA[l, f])
                slot += DOWN_SLOTS
                chunk += DOWN_ADA[l, f]
                ffn += 1
            tile += KD
    assert slot == SLOTS and chunk == CHUNKS
    return at


AT = schedule()


def build(nc, x_t, params, ada_w, weights, gate_w, sgu_w, sgu_b, out):
    with ExitStack() as ctx:
        def sb(name, shape, dt=F32, scope=ctx):
            return scope.enter_context(nc.sbuf_tensor(name, shape, dt))

        def sem(name):
            return ctx.enter_context(nc.semaphore(name))

        res = sb("res", [P, KD, T])
        z_hi = sb("z_hi", [P, KD, T], F32R)
        z_lo = sb("z_lo", [P, KD, T], F32R)
        raw = sb("raw", [P, RING, SLOT])
        w_hi = sb("w_hi", [P, RING, SLOT], F32R)
        w_lo = sb("w_lo", [P, RING, SLOT], F32R)
        ada_raw = sb("ada_raw", [P, ADA_RING, 4, 256])
        ada_rows = sb("ada_rows", [P, 512])
        scr = sb("scr", [P, 3, T])
        mods = sb("mods", [P, DEPTH * NMOD * KD, 2])
        n_gain = sb("n_gain", [P, DEPTH * 3, KD, 2])
        n_shift = sb("n_shift", [P, DEPTH * 3, KD, 2])
        gates = sb("gates", [P, DEPTH * 3, KD, 2])
        par = sb("par", [P, N_PAR])
        c_cols = sb("c_cols", [P, KD, 32])
        ident = sb("ident", [P, P])
        ones = sb("ones", [P, P])
        lam_t = sb("lam_t", [P, 6, DEPTH * 2 * LT])
        half_b = sb("half_b", [P, 2, DEPTH * 2 * LT])
        tok = sb("tok", [P, 4])
        tokr = sb("tokr", [P, 4])
        mhalf = sb("mhalf", [P, 4])
        bn6 = sb("bn6", [P, 4, 6])
        bn2 = sb("bn2", [P, 4, 2])

        with ExitStack() as ffn_scope:
            h_hi = sb("h_hi", [P, KF, T], F32R, ffn_scope)
            h_lo = sb("h_lo", [P, KF, T], F32R, ffn_scope)
        xpad = sb("xpad", [P, 2, 2, SEQ + 3])
        xc = sb("xc", [P, LT, T])
        l_s = sb("l_s", [P, 4, T])
        l_q = sb("l_q", [P, 4, T])
        l_bx = sb("l_bx", [P, 4, T])
        l_a = sb("l_a", [P, 4, T])
        y_lru = sb("y_lru", [P, LT, T])
        gl = sb("gl", [P, LT, T])
        v_n = sb("v_n", [P, 4, 512])
        y_sgu = sb("y_sgu", [P, LT, T])
        bd = sb("bd", [P, 16, P])
        ws = sb("ws", [P, LT, P])
        bs = sb("bs", [P, LT, P])

        bank = [ctx.enter_context(nc.psum_tensor(f"bank{i}", [P, 512], F32)) for i in range(8)]
        pa, po, p_ada, p_misc = bank[0:4], bank[4:6], bank[6], bank[7]

        raw_in = [sem(f"raw_in{i}") for i in range(RING)]
        ada_in = [sem(f"ada_in{i}") for i in range(ADA_RING)]
        hi_ready, lo_ready, slot_done = sem("hi_ready"), sem("lo_ready"), sem("slot_done")
        ada_used, rows_ready = sem("ada_used"), sem("rows_ready")
        rows_turned, mods_ready = sem("rows_turned"), sem("mods_ready")
        par_in, x_in, out_done, mix_in = sem("par_in"), sem("x_in"), sem("out_done"), sem("mix_in")
        const_ready, cvec_ready = sem("const_ready"), sem("cvec_ready")
        prepped, pool_chain, dve_chain, act_chain = sem("prepped"), sem("pool_chain"), sem("dve_chain"), sem("act_chain")
        silu_ready, hid_ready = sem("silu_ready"), sem("hid_ready")
        hid_hi_ready, hid_lo_ready = sem("hid_hi_ready"), sem("hid_lo_ready")
        res_ready, sq_ready, sqsum_ready = sem("res_ready"), sem("sq_ready"), sem("sqsum_ready")
        ss_done, var_ready, rstd_ready = sem("ss_done"), sem("var_ready"), sem("rstd_ready")
        diag_ready, bcast_done = sem("diag_ready"), sem("bcast_done")
        zt_ready, z_hi_ready, z_ready = sem("zt_ready"), sem("z_hi_ready"), sem("z_ready")
        copy_ready, xc_ready, gate_mm = sem("copy_ready"), sem("xc_ready"), sem("gate_mm")
        ti_ready, exp_ready, bx_ready = sem("ti_ready"), sem("exp_ready"), sem("bx_ready")
        a_ready, sqrt_ready, scan_ready = sem("a_ready"), sem("sqrt_ready"), sem("scan_ready")
        gelu_ready, vvar_ready, vrstd_ready = sem("gelu_ready"), sem("vvar_ready"), sem("vrstd_ready")
        vn_ready, spatial_mm, zz_ready = sem("vn_ready"), sem("spatial_mm"), sem("zz_ready")
        y_ready, y_hi_ready = sem("y_ready"), sem("y_hi_ready")
        y_lo_dve, y_lo_pool = sem("y_lo_dve"), sem("y_lo_pool")
        lam_ready, bd_zero = sem("lam_ready"), sem("bd_zero")
        block = ctx.enter_context(nc.Block())

        HID0 = 2
        HID_LO0 = 1

        def dft(n):
            return SEQ if n >= 5 else T

        def streams(width):
            return 1 if width == SEQ else 2

        @block.sync
        def _(sp):
            def slot_dma(s, r):
                if isinstance(s, int) and s >= SLOTS:
                    return
                if not isinstance(s, int) or s >= RING:
                    sp.wait_ge(lo_ready, s - (RING - 1))
                src = weights[s] if isinstance(s, int) else weights[bass.ds(s, 1)].rearrange("a p n -> p (a n)")
                sp.dma_start(raw[:, r, :], src).then_inc(raw_in[r], 16)

            def unit_dma(u, r):
                if isinstance(u, int) and u >= UNITS:
                    return
                if not isinstance(u, int) or u >= ADA_RING:
                    sp.wait_ge(ada_used, u - (ADA_RING - 1))
                src = ada_w[u] if isinstance(u, int) else ada_w[bass.ds(u, 1)].rearrange("a p n -> p (a n)")
                sp.dma_start(ada_raw[:, r, :, :].rearrange("p a n -> p (a n)"), src).then_inc(ada_in[r], 16)

            def stage(base, unit=None):
                def body(i):
                    for q in range(4):
                        slot_dma(base + 8 + i * 4 + q, q)
                        if unit is not None:
                            unit_dma(unit + 2 + i * 4 + q, q % 2)
                return body

            def run(body, n, peel):
                if n - peel > 0:
                    with sp.Fori(0, n - peel) as i:
                        body(i)
                for i in range(n - peel, n):
                    body(i)

            sp.dma_start(par[:], params).then_inc(par_in, 16)
            unit_dma(0, 0)
            unit_dma(1, 1)
            sp.dma_start(res[:], x_t).then_inc(x_in, 16)
            for u in range(2, 4 * HEAD_CHUNKS + 2):
                unit_dma(u, u % 2)
                if u % 4 == 3:
                    slot_dma(u // 4, u // 4)
            for s in range(RING, 8):
                slot_dma(s, s % RING)
            for l in range(DEPTH):
                for f in range(2):
                    up, down = AT[l, "up", f], AT[l, "down", f]
                    n_ada = up["ada"]
                    if n_ada:
                        last = up["chunk"] + n_ada == CHUNKS
                        run(stage(up["slot"], 4 * up["chunk"]), n_ada, 1 if last else 0)
                    if n_ada < UP_SLOTS // 4:
                        run(stage(up["slot"] + 4 * n_ada), UP_SLOTS // 4 - n_ada, 0)
                    final = l == DEPTH - 1 and f == 1
                    run(stage(down["slot"], 4 * down["chunk"] if down["ada"] else None),
                        DOWN_SLOTS // 4, 2 if final else 0)
                    if f == 0:
                        sp.wait_ge(slot_done, AT[l, "in"]["slot"])
                        sp.wait_ge(bd_zero, l + 1)
                        for a in range(2):
                            sp.dma_start(bd[64 * a:64 * a + 64, :, 64 * a:64 * a + 64], gate_w[l, a]).then_inc(mix_in, 16)
                        sp.dma_start(ws[:], sgu_w[l]).then_inc(mix_in, 16)
                        sp.dma_start(bs[:], sgu_b[l].partition_broadcast(P)).then_inc(mix_in, 16)
                        run(stage(AT[l, "in"]["slot"]), (IN_SLOTS + OUT_SLOTS) // 4, 0)
            for k in range(KD):
                sp.wait_ge(zt_ready, 6 * KD + k + 1)
                sp.dma_start(out[k], res[:, k, 0:SEQ]).then_inc(out_done, 16)
            sp.wait_ge(out_done, 16 * KD)

        @block.tensor
        def _(pe):
            def product(bank_ap, blk, r, rhs_hi, rhs_lo, start, stop):
                c = slice(blk * P, (blk + 1) * P)
                pe.matmul(bank_ap, w_hi[:, r, c], rhs_hi, start=start, stop=False)
                pe.matmul(bank_ap, w_hi[:, r, c], rhs_lo, start=False, stop=False)
                return pe.matmul(bank_ap, w_lo[:, r, c], rhs_hi, start=False, stop=stop)

            def ada_main(c, q):
                if q == 0:
                    if not isinstance(c, int) or c > 0:
                        pe.wait_ge(rows_ready, c)
                    if isinstance(c, int) and c == 0:
                        pe.wait_ge(cvec_ready, 1)
                pe.wait_ge(ada_in[q % 2], (c * 2 + q // 2 + 1) * 16)
                half, kh = q // 2, q % 2
                for j in range(4):
                    m = pe.matmul(p_ada[32 * j:32 * j + 32, half * 256:half * 256 + 256],
                                  c_cols[:, kh * 4 + j, :], ada_raw[:, q % 2, j, :],
                                  start=(kh == 0), stop=(kh == 1), tile_position=(0, 32 * j))
                m.then_inc(ada_used, 1)

            def ada_turn(c):
                pe.wait_ge(rows_ready, c + 1)
                if not isinstance(c, int) or c > 0:
                    pe.wait_ge(mods_ready, c)
                if isinstance(c, int) and c == 0:
                    pe.wait_ge(const_ready, 1)
                for q in range(4):
                    m = pe.transpose(p_misc[:, q * P:(q + 1) * P], ada_rows[:, q * P:(q + 1) * P], ident[:])
                m.then_inc(rows_turned, 1)

            def norm(n):
                w = dft(n)
                if n == 0:
                    pe.wait_ge(const_ready, 1)
                pe.wait_ge(sqsum_ready, 6 * (n + 1))
                pe.wait_ge(res_ready, HID0 + KD * n)
                for src in (2, 1):
                    if src == 1:
                        pe.wait_ge(sq_ready, KD * (n + 1))
                    for m in range(w // P):
                        mm = pe.matmul(po[0][:, m:m + 1], scr[:, src, m * P:(m + 1) * P], ones[:, 0:1],
                                       start=(src == 2 and m == 0), stop=(src == 1), skip_group_check=True)
                mm.then_inc(ss_done, 1)
                pe.wait_ge(diag_ready, n + 1)
                pe.matmul(po[1][:, 0:w], ones[:], scr[:, 0, 0:w], start=True, stop=True).then_inc(bcast_done, 1)

            def up_stage(l, f):
                at = AT[l, "up", f]
                n = 3 * l + 2 * f
                w = dft(n)

                def body(i, ada):
                    for q in range(4):
                        s = at["slot"] + i * 4 + q
                        j2 = at["ffn"] * KF + i * 2 + q // 2
                        pe.wait_ge(lo_ready, s + 1)
                        if q % 2 == 0:
                            pe.wait_ge(hid_ready, HID0 - 1 + j2)
                        for k in range(KD):
                            if q == 0:
                                pe.wait_ge(z_ready, KD * n + k + 1)
                            m = product(pa[q][:, 0:w], k, q, z_hi[:, k, 0:w], z_lo[:, k, 0:w], k == 0, k == KD - 1)
                        m.then_inc(slot_done, 1)
                        if ada:
                            ada_main(at["chunk"] + i, q)
                    if ada:
                        ada_turn(at["chunk"] + i)

                if at["ada"]:
                    with pe.Fori(0, at["ada"]) as i:
                        body(i, True)
                if at["ada"] < UP_SLOTS // 4:
                    with pe.Fori(at["ada"], UP_SLOTS // 4) as i:
                        body(i, False)

            def down_stage(l, f):
                at = AT[l, "down", f]
                w = dft(3 * l + 2 * f)
                with pe.Fori(0, 2) as i:
                    for dd in range(4):
                        for part, n_blk in enumerate((8, 8, 6)):
                            q = 3 * dd + part
                            pe.wait_ge(lo_ready, at["slot"] + 1 + i * 12 + q)
                            if part == 0:
                                pe.wait_ge(res_ready, HID0 - 1 + at["tile"] + i * 4 + dd)
                            for b in range(n_blk):
                                k = 8 * part + b
                                if dd == 0 and k in (0, KF - 2, KF - 1):
                                    pe.wait_ge(hid_lo_ready, HID_LO0 + at["ffn"] * KF + max(k + 1, KF - 2))
                                m = product(po[dd % 2][:, 0:w], b, q % RING, h_hi[:, k, 0:w], h_lo[:, k, 0:w],
                                            k == 0, k == KF - 1)
                            m.then_inc(slot_done, 1)
                            if at["ada"]:
                                c = at["chunk"] + i * 3 + q // 4
                                ada_main(c, q % 4)
                                if q % 4 == 3:
                                    ada_turn(c)

            def in_stage(l):
                at = AT[l, "in"]
                n = 3 * l + 1
                wl = SEQ if l == DEPTH - 1 else T
                for q in range(IN_SLOTS):
                    pe.wait_ge(lo_ready, at["slot"] + q + 1)
                    kind, t = q // 4, q % 4
                    if kind in (0, 2):
                        if q == 1:
                            pe.wait_ge(zt_ready, KD * (n + 1))
                        elif q:
                            pe.wait_ge(copy_ready, 8 * l + (t - 1 if kind == 0 else t + 3))
                    if q == 4:
                        pe.wait_ge(hid_ready, HID0 + KF * (2 * l + 1))
                    if q == 12:
                        pe.wait_ge(vn_ready, l + 1)
                    w = T if kind == 0 else wl
                    if kind == 1:
                        for kk in range(2):
                            k = 2 * t + kk
                            c = slice(kk * 512, kk * 512 + 512)
                            for m_ in range(wl // P):
                                tk = slice(m_ * P, m_ * P + P)
                                pe.matmul(pa[m_][:], z_hi[:, k, tk], w_hi[:, q % 4, c], start=(k == 0), stop=False)
                                pe.matmul(pa[m_][:], z_lo[:, k, tk], w_hi[:, q % 4, c], start=False, stop=False)
                                m = pe.matmul(pa[m_][:], z_hi[:, k, tk], w_lo[:, q % 4, c], start=False, stop=(k == KD - 1))
                    else:
                        dst = pa[t] if kind == 3 else po[t % 2]
                        for k in range(KD):
                            if q == 0:
                                pe.wait_ge(z_ready, KD * n + k + 1)
                            m = product(dst[:, 0:w], k, q % 4, z_hi[:, k, 0:w], z_lo[:, k, 0:w], k == 0, k == KD - 1)
                    m.then_inc(slot_done, 1)
                    if 4 <= q < 12:
                        u = q - 4
                        t_, d_ = u // 2, u % 2
                        pe.wait_ge(xc_ready, 4 * l + t_ + 1)
                        if u == 0:
                            pe.wait_ge(mix_in, 64 * (l + 1))
                            pe.wait_ge(mods_ready, at["chunk"])
                            pe.wait_ge(rows_ready, at["chunk"])
                        if u or l:
                            pe.wait_ge(ti_ready, 8 * l + u)
                        for kind_, dst in ((0, p_ada), (1, p_misc)):
                            m = pe.matmul(dst[:], bd[:, kind_ * 8 + d_ * 4 + t_, :], xc[:, t_, :], start=True, stop=True)
                        m.then_inc(gate_mm, 1)
                    if q >= 12:
                        g = q - 12
                        if g < 2:
                            pe.wait_ge(ti_ready, 8 * (l + 1))
                        else:
                            pe.wait_ge(zz_ready, 4 * l + g - 1)
                        dst = (p_ada, p_misc)[g % 2]
                        for m_ in range(wl // P):
                            m = pe.matmul(dst[:, m_ * P:(m_ + 1) * P], v_n[:, m_, g * P:(g + 1) * P], ws[:, g, :],
                                          start=True, stop=True)
                        m.then_inc(spatial_mm, 1)

            def out_stage(l):
                at = AT[l, "out"]
                w = SEQ if l == DEPTH - 1 else T
                with pe.Fori(0, 2) as i:
                    for q in range(4):
                        pe.wait_ge(lo_ready, at["slot"] + 1 + i * 4 + q)
                        pe.wait_ge(res_ready, HID0 - 1 + at["tile"] + i * 4 + q)
                        if q < 2:
                            pe.wait_ge(copy_ready, 8 * (l + 1))
                        for k in range(KD):
                            if q == 0:
                                pe.wait_ge(y_lo_dve if k % 2 == 0 else y_lo_pool, 4 * l + k // 2 + 1)
                            m = product(po[q % 2][:, 0:w], k, q, z_hi[:, k, 0:w], z_lo[:, k, 0:w], k == 0, k == KD - 1)
                        m.then_inc(slot_done, 1)

            for c in range(HEAD_CHUNKS):
                for q in range(4):
                    ada_main(c, q)
                if c:
                    ada_turn(c - 1)
            ada_turn(HEAD_CHUNKS - 1)
            norm(0)
            for l in range(DEPTH):
                up_stage(l, 0)
                down_stage(l, 0)
                norm(3 * l + 1)
                in_stage(l)
                out_stage(l)
                norm(3 * l + 2)
                up_stage(l, 1)
                down_stage(l, 1)
                norm(3 * l + 3)

        @block.scalar
        def _(act):
            def split_hi(s, r):
                if isinstance(s, int) and s >= SLOTS:
                    return
                if isinstance(s, int):
                    act.wait_ge(raw_in[r], 16 * (s // RING + 1))
                act.activation(w_hi[:, r, :], raw[:, r, :], ACT.Copy).then_inc(hi_ready, 1)

            def hi_in_loop(base, i, per, q):
                r = q % RING
                act.wait_ge(raw_in[r], 16 * ((base + q) // RING + 2) + i * (16 * per // RING))
                act.activation(w_hi[:, r, :], raw[:, r, :], ACT.Copy).then_inc(hi_ready, 1)

            def square(d, n):
                w = dft(n)
                if n:
                    act.wait_ge(res_ready, HID0 + KD * (n - 1) + d + 1)
                if d >= 3:
                    act.wait_ge(sqsum_ready, 6 * n + d - 2)
                dst = 2 if d == 0 else d % 2
                act.activation(scr[:, dst, 0:w], res[:, d, 0:w], ACT.Square).then_inc(sq_ready, 1)

            def norm(n):
                if n == 3 * DEPTH:
                    return
                w = dft(n)
                for k in range(KD):
                    act.wait_ge(zt_ready, KD * n + k + 1)
                    act.activation(z_hi[:, k, 0:w], scr[:, k % 3, 0:w], ACT.Copy).then_inc(z_hi_ready, 1)

            def up_stage(l, f):
                at = AT[l, "up", f]
                w = dft(3 * l + 2 * f)
                with act.Fori(0, UP_SLOTS // 4) as i:
                    for q in range(4):
                        j = at["ffn"] * KF + i * 2 + q // 2
                        act.wait_ge(slot_done, at["slot"] + 1 + i * 4 + q)
                        if q % 2 == 0:
                            act.activation(scr[:, q // 2, 0:w], pa[q][:, 0:w], ACT.Silu).then_inc(silu_ready, 1)
                            hi_in_loop(at["slot"], i, 4, q)
                        else:
                            hi_in_loop(at["slot"], i, 4, q)
                            act.wait_ge(hid_ready, HID0 + 1 + j)
                            act.activation(h_hi[:, bass.ds(i * 2 + q // 2, 1), 0:w].rearrange("p a n -> p (a n)"),
                                           scr[:, 2, 0:w], ACT.Copy).then_inc(hid_hi_ready, 1)

            def down_stage(l, f):
                at = AT[l, "down", f]
                for q in range(DOWN_SLOTS):
                    act.wait_ge(slot_done, at["slot"] + q + 1)
                    split_hi(at["slot"] + q + 4, q % 4)
                    if q % 3 == 2:
                        square(q // 3, 3 * l + 2 * f + 1)

            def in_stage(l):
                at = AT[l, "in"]
                wl = SEQ if l == DEPTH - 1 else T
                ns = wl // SEQ
                for q in range(IN_SLOTS):
                    act.wait_ge(slot_done, at["slot"] + q + 1)
                    kind, t = q // 4, q % 4
                    if kind == 0:
                        if t >= 2:
                            act.wait_ge(xc_ready, 4 * l + t - 1)
                        elif t == 0:
                            act.wait_ge(bd_zero, l + 1)
                        act.activation(xpad[:, t % 2, :, 2:2 + SEQ], po[t % 2].rearrange("p (s n) -> p s n", s=2),
                                       ACT.Copy).then_inc(copy_ready, 1)
                    if kind == 2:
                        act.activation(gl[:, t, 0:wl], po[t % 2][:, 0:wl], ACT.Copy).then_inc(copy_ready, 1)
                    split_hi(at["slot"] + q + 4, q % 4)
                    if q in (7, 9, 11, 13):
                        t_ = (q - 7) // 2
                        for u in (2 * t_, 2 * t_ + 1):
                            act.wait_ge(a_ready, 8 * l + u + 1)
                            act.activation(l_s[:, u % 4, :], l_s[:, u % 4, :], ACT.Sqrt).then_inc(sqrt_ready, 1)
                    if 4 <= q < 12:
                        u = q - 4
                        t_, d_ = u // 2, u % 2
                        c = l * 8 + d_ * 4 + t_
                        r = u % 4
                        act.wait_ge(gate_mm, 8 * l + u + 1)
                        if u >= 4:
                            act.wait_ge(scan_ready, 4 * l + t_ - 1)
                        elif u == 0:
                            act.wait_ge(lam_ready, 3)
                        act.activation(l_q[:, r, :], p_ada[:], ACT.Tanh, bias=half_b[:, 0, c:c + 1], scale=0.5).then_inc(act_chain, 1)
                        act.activation(l_bx[:, r, :], p_misc[:], ACT.Tanh, bias=half_b[:, 1, c:c + 1], scale=0.5).then_inc(ti_ready, 1)
                        act.wait_ge(act_chain, 2 * (8 * l + u) + 1)
                        act.activation(l_s[:, r, :], l_q[:, r, :], ACT.Tanh, bias=lam_t[:, 4, c:c + 1],
                                       scale=lam_t[:, 4, c:c + 1]).then_inc(act_chain, 1)
                        act.activation(l_q[:, r, :], l_q[:, r, :], ACT.Exp, bias=lam_t[:, 5, c:c + 1],
                                       scale=lam_t[:, 5, c:c + 1]).then_inc(exp_ready, 1)
                    if q == 14:
                        for t_ in range(LT):
                            act.wait_ge(copy_ready, 8 * (l + 1))
                            act.activation(gl[:, t_, 0:wl], gl[:, t_, 0:wl], ACT.Gelu_apprx_tanh).then_inc(gelu_ready, 1)
                for k in range(KD):
                    act.wait_ge(y_ready, 8 * l + k + 1)
                    src = y_lru if k < 4 else y_sgu
                    act.activation(z_hi[:, k, 0:wl], src[:, k % 4, 0:wl], ACT.Copy).then_inc(y_hi_ready, 1)

            def out_stage(l):
                at = AT[l, "out"]
                for q in range(OUT_SLOTS):
                    act.wait_ge(slot_done, at["slot"] + q + 1)
                    split_hi(at["slot"] + q + 4, q % 4)
                    square(q, 3 * l + 2)

            act.wait_ge(par_in, 16)
            act.wait_ge(const_ready, 1)
            act.activation(c_cols[:, :, 0:2], par[:, C_CVEC:C_CVEC + 2 * KD].rearrange("p (k s) -> p k s", s=2),
                           ACT.Silu).then_inc(cvec_ready, 1)
            act.wait_ge(lam_ready, 1)
            act.activation(lam_t[:, 1, :], lam_t[:, 0, :], ACT.Exp, scale=-1.0).then_inc(lam_ready, 1)
            act.wait_ge(x_in, 16)
            for d in range(KD):
                square(d, 0)
            for s in range(RING):
                split_hi(s, s)
            norm(0)
            for l in range(DEPTH):
                up_stage(l, 0)
                down_stage(l, 0)
                norm(3 * l + 1)
                in_stage(l)
                out_stage(l)
                norm(3 * l + 2)
                up_stage(l, 1)
                down_stage(l, 1)
                norm(3 * l + 3)

        @block.vector
        def _(dve):
            chain = [0]

            def link(ins):
                chain[0] += 1
                ins.then_inc(dve_chain, 1)
                dve.wait_ge(dve_chain, chain[0])

            def split_lo(s, r):
                if isinstance(s, int) and s >= SLOTS:
                    return
                dve.wait_ge(hi_ready, s + 1)
                dve.tensor_tensor(w_lo[:, r, :], raw[:, r, :], w_hi[:, r, :].bitcast(F32), ALU.subtract).then_inc(lo_ready, 1)

            def ada_copy(c):
                dve.wait_ge(ada_used, c * 4 + 4)
                if not isinstance(c, int) or c > 0:
                    dve.wait_ge(rows_turned, c)
                dve.tensor_copy(ada_rows[:], p_ada[:]).then_inc(rows_ready, 1)

            def ada_sum(c):
                dve.wait_ge(rows_turned, c + 1)
                src = p_misc.rearrange("p (t j r) -> p t r j", t=4, j=4)[:, :, 0:2, :]
                dst = mods[:, c * 4:c * 4 + 4, :] if isinstance(c, int) else mods[:, bass.ds(c * 4, 4), :]
                dve.tensor_reduce(dst, src, AX_X, ALU.add).then_inc(mods_ready, 1)

            def residual(l, norm_i, d, w, tile):
                if d == 0:
                    dve.wait_ge(prepped, 6 * l + 2 * norm_i + 2)
                for s in range(streams(w)):
                    c = slice(s * SEQ, (s + 1) * SEQ)
                    m = dve.scalar_tensor_tensor(res[:, d, c], po[d % 2][:, c], gates[:, 3 * l + norm_i, d, s:s + 1],
                                                 res[:, d, c], ALU.mult, ALU.add)
                m.then_inc(res_ready, 1)

            def norm(n):
                w = dft(n)
                m4 = w // P
                dve.wait_ge(ss_done, n + 1)
                dve.tensor_scalar(tok[:, 0:m4], po[0][:, 0:m4], 1.0 / D, EPS, ALU.mult, ALU.add).then_inc(var_ready, 1)
                dve.wait_ge(rstd_ready, n + 1)
                dve.tensor_tensor(scr[:, 0, 0:w].rearrange("p (m j) -> p m j", j=P),
                                  ident[:].unsqueeze(1).to_broadcast([P, m4, P]),
                                  tokr[:, 0:m4].unsqueeze(2).to_broadcast([P, m4, P]), ALU.mult).then_inc(diag_ready, 1)
                dve.wait_ge(bcast_done, n + 1)
                if n < 3 * DEPTH:
                    dve.wait_ge(prepped, 2 * n + 1)
                for k in range(KD):
                    if n == 3 * DEPTH:
                        link(dve.tensor_tensor(scr[:, k % 3, 0:w], res[:, k, 0:w], po[1][:, 0:w], ALU.mult))
                        g = C_GAIN + n * KD + k
                        dve.tensor_scalar(res[:, k, 0:w], scr[:, k % 3, 0:w], par[:, g:g + 1], None, ALU.mult).then_inc(zt_ready, 1)
                        continue
                    if k >= 3:
                        dve.wait_ge(z_ready, KD * n + k - 2)
                    link(dve.tensor_tensor(scr[:, k % 3, 0:w], res[:, k, 0:w], po[1][:, 0:w], ALU.mult))
                    for s in range(streams(w)):
                        c = slice(s * SEQ, (s + 1) * SEQ)
                        m = dve.tensor_scalar(scr[:, k % 3, c], scr[:, k % 3, c], n_gain[:, n, k, s:s + 1],
                                              n_shift[:, n, k, s:s + 1], ALU.mult, ALU.add)
                    m.then_inc(zt_ready, 1)

            def up_stage(l, f):
                at = AT[l, "up", f]
                w = dft(3 * l + 2 * f)

                def body(i, ada):
                    for q in range(4):
                        s = at["slot"] + i * 4 + q
                        j = at["ffn"] * KF + i * 2 + q // 2
                        dve.wait_ge(slot_done, s + 1)
                        if q % 2 == 1:
                            dve.wait_ge(silu_ready, j + 1)
                            dve.wait_ge(hid_lo_ready, HID_LO0 + j)
                            dve.tensor_tensor(scr[:, 2, 0:w], scr[:, q // 2, 0:w], pa[q][:, 0:w], ALU.mult).then_inc(hid_ready, 1)
                        split_lo(s + 4, q)
                        if q % 2 == 1:
                            dve.wait_ge(hid_hi_ready, j + 1)
                            jj = bass.ds(i * 2 + q // 2, 1)
                            dve.tensor_tensor(h_lo[:, jj, 0:w].rearrange("p a n -> p (a n)"), scr[:, 2, 0:w],
                                              h_hi[:, jj, 0:w].rearrange("p a n -> p (a n)").bitcast(F32),
                                              ALU.subtract).then_inc(hid_lo_ready, 1)
                    if ada:
                        ada_copy(at["chunk"] + i)
                        ada_sum(at["chunk"] + i)

                if at["ada"]:
                    with dve.Fori(0, at["ada"]) as i:
                        body(i, True)
                if at["ada"] < UP_SLOTS // 4:
                    with dve.Fori(at["ada"], UP_SLOTS // 4) as i:
                        body(i, False)

            def down_stage(l, f):
                at = AT[l, "down", f]
                w = dft(3 * l + 2 * f)
                for q in range(DOWN_SLOTS):
                    dve.wait_ge(slot_done, at["slot"] + q + 1)
                    if q % 3 == 2:
                        residual(l, 2 * f, q // 3, w, at["tile"])
                    split_lo(at["slot"] + q + 4, q % 4)
                    if at["ada"] and q % 4 == 3:
                        ada_copy(at["chunk"] + q // 4)
                        ada_sum(at["chunk"] + q // 4)

            def conv(l, t):
                dve.wait_ge(copy_ready, 8 * l + t + 1)
                o = xc[:, t, :].rearrange("p (s n) -> p s n", s=2)
                c = C_CONV + l * 5 * LT + t
                link(dve.tensor_scalar(o, xpad[:, t % 2, :, 0:SEQ], par[:, c:c + 1], par[:, c + 4 * LT:c + 4 * LT + 1],
                                       ALU.mult, ALU.add))
                for k in range(1, 4):
                    m = dve.scalar_tensor_tensor(o, xpad[:, t % 2, :, k:k + SEQ], par[:, c + k * LT:c + k * LT + 1], o,
                                                 ALU.mult, ALU.add)
                    if k < 3:
                        link(m)
                m.then_inc(xc_ready, 1)

            def decay(l, u):
                r = u % 4
                dve.wait_ge(exp_ready, 8 * l + u + 1)
                link(dve.tensor_scalar(l_a[:, r, :], l_q[:, r, :], 1.0, None, ALU.add))
                link(dve.scalar_tensor_tensor(l_q[:, r, :], l_s[:, r, :], 1.0, l_a[:, r, :], ALU.add, ALU.mult))
                link(dve.tensor_scalar(l_q[:, r, :], l_q[:, r, :], 0.25, -1.0, ALU.mult, ALU.add))
                link(dve.tensor_tensor(l_q[:, r, :], l_a[:, r, :], l_q[:, r, :], ALU.mult))
                dve.scalar_tensor_tensor(l_a[:, r, :], l_s[:, r, :], -1.0, l_q[:, r, :], ALU.add, ALU.mult).then_inc(a_ready, 1)

            def scans(l, t):
                for d in range(2):
                    u = 2 * t + d
                    r = u % 4
                    dve.wait_ge(sqrt_ready, 8 * l + u + 1)
                    link(dve.tensor_tensor(l_q[:, r, :], l_s[:, r, :], l_q[:, r, :], ALU.mult))
                    dve.wait_ge(bx_ready, 8 * l + u + 1)
                    link(dve.scalar_tensor_tensor(l_q[:, r, :], l_q[:, r, :], -1.0, l_bx[:, r, :], ALU.mult, ALU.mult))
                    if d == 0:
                        link(dve.tensor_tensor_scan(l_bx[:, r, SEQ:T], l_a[:, r, SEQ:T], l_q[:, r, SEQ:T], 0.0,
                                                    ALU.mult, ALU.add))
                        link(dve.tensor_tensor_scan(l_bx[:, r, 0:SEQ], l_a[:, r, 0:SEQ], l_q[:, r, 0:SEQ],
                                                    l_bx[:, r, T - 1:T], ALU.mult, ALU.add))
                    else:
                        link(dve.tensor_tensor_scan(l_bx[:, r, ::-1], l_a[:, r, ::-1], l_q[:, r, ::-1], 0.0,
                                                    ALU.mult, ALU.add))
                r0 = (2 * t) % 4
                dve.tensor_tensor(y_lru[:, t, :], l_bx[:, r0, :], l_bx[:, r0 + 1, :], ALU.add).then_inc(scan_ready, 1)

            def in_stage(l):
                at = AT[l, "in"]
                wl = SEQ if l == DEPTH - 1 else T
                m4 = wl // P
                for q in range(IN_SLOTS):
                    dve.wait_ge(slot_done, at["slot"] + q + 1)
                    split_lo(at["slot"] + q + 4, q % 4)
                    if q < 4:
                        conv(l, q)
                    if 5 <= q < 13:
                        decay(l, q - 5)
                    if q == 7:
                        for m_ in range(m4):
                            m = dve.bn_stats(bn6[:, m_, :], pa[m_][:])
                        link(m)
                        for m_ in range(m4):
                            m = dve.bn_aggr(bn2[:, m_, :], bn6[:, m_, :])
                        m.then_inc(vvar_ready, 1)
                    if q == 9:
                        dve.wait_ge(vrstd_ready, l + 1)
                        for m_ in range(m4):
                            m = dve.tensor_scalar(v_n[:, m_, :], pa[m_][:], bn2[:, m_, 0:1], tokr[:, m_:m_ + 1],
                                                  ALU.subtract, ALU.mult)
                        m.then_inc(vn_ready, 1)
                    if q in (8, 10, 12, 14):
                        scans(l, (q - 8) // 2)
                    if q >= 12:
                        g = q - 12
                        dve.wait_ge(spatial_mm, 4 * l + g + 1)
                        src = (p_ada, p_misc)[g % 2][:, 0:wl].rearrange("p (m j) -> p m j", j=P)
                        o = y_sgu[:, g, 0:wl].rearrange("p (m j) -> p m j", j=P)
                        c = C_SGU + l * LT + g
                        if g == 0:
                            dve.wait_ge(mix_in, 64 * (l + 1))
                        dve.scalar_tensor_tensor(o, src, par[:, c:c + 1], bs[:, g, :].unsqueeze(1).to_broadcast([P, m4, P]),
                                                 ALU.mult, ALU.add).then_inc(zz_ready, 1)
                for k in range(KD):
                    if k < 4:
                        dve.wait_ge(gelu_ready, 4 * l + k + 1)
                        dve.wait_ge(scan_ready, 4 * l + k + 1)
                        dve.tensor_tensor(y_lru[:, k, 0:wl], y_lru[:, k, 0:wl], gl[:, k, 0:wl], ALU.mult).then_inc(y_ready, 1)
                    else:
                        dve.wait_ge(zz_ready, 4 * l + k - 3)
                        dve.tensor_tensor(y_sgu[:, k - 4, 0:wl], y_sgu[:, k - 4, 0:wl], pa[k - 4][:, 0:wl], ALU.mult).then_inc(y_ready, 1)
                    if k % 2 == 1:
                        kk = k - 1
                        src = y_lru if kk < 4 else y_sgu
                        dve.wait_ge(y_hi_ready, 8 * l + kk + 1)
                        dve.tensor_tensor(z_lo[:, kk, 0:wl], src[:, kk % 4, 0:wl], z_hi[:, kk, 0:wl].bitcast(F32),
                                          ALU.subtract).then_inc(y_lo_dve, 1)

            def out_stage(l):
                at = AT[l, "out"]
                w = SEQ if l == DEPTH - 1 else T
                for q in range(OUT_SLOTS):
                    dve.wait_ge(slot_done, at["slot"] + q + 1)
                    residual(l, 1, q, w, at["tile"])
                    split_lo(at["slot"] + q + 4, q % 4)

            def softplus():
                lam = par[:, C_LAM:C_LAM + DEPTH * 2 * LT]
                link(dve.tensor_scalar(lam_t[:, 0, :], lam, -1.0, None, ALU.mult))
                dve.tensor_tensor(lam_t[:, 0, :], lam_t[:, 0, :], lam, ALU.max).then_inc(lam_ready, 1)
                dve.wait_ge(lam_ready, 2)
                link(dve.tensor_scalar(lam_t[:, 2, :], lam_t[:, 1, :], 2.0, None, ALU.add))
                link(dve.reciprocal(lam_t[:, 2, :], lam_t[:, 2, :]))
                link(dve.tensor_tensor(lam_t[:, 1, :], lam_t[:, 1, :], lam_t[:, 2, :], ALU.mult))
                link(dve.tensor_tensor(lam_t[:, 2, :], lam_t[:, 1, :], lam_t[:, 1, :], ALU.mult))
                link(dve.tensor_scalar(lam_t[:, 3, :], lam_t[:, 2, :], 1.0 / 17, None, ALU.mult))
                for c in range(15, 1, -2):
                    link(dve.scalar_tensor_tensor(lam_t[:, 3, :], lam_t[:, 3, :], 1.0 / c, lam_t[:, 2, :], ALU.add, ALU.mult))
                link(dve.scalar_tensor_tensor(lam_t[:, 3, :], lam_t[:, 3, :], 1.0, lam_t[:, 1, :], ALU.add, ALU.mult))
                link(dve.tensor_scalar(lam_t[:, 0, :], lam, -1.0, 0.0, ALU.mult, ALU.max))
                link(dve.scalar_tensor_tensor(lam_t[:, 3, :], lam_t[:, 3, :], 2.0, lam_t[:, 0, :], ALU.mult, ALU.add))
                dve.tensor_scalar(lam_t[:, 4, :], lam_t[:, 3, :], 2.0, None, ALU.mult)
                dve.tensor_scalar(lam_t[:, 5, :], lam_t[:, 3, :], -4.0, None, ALU.mult)
                dve.tensor_scalar(half_b[:, 0, :], par[:, C_BR:C_BR + DEPTH * 2 * LT], 0.5, None, ALU.mult)
                dve.tensor_scalar(half_b[:, 1, :], par[:, C_BI:C_BI + DEPTH * 2 * LT], 0.5, None, ALU.mult).then_inc(lam_ready, 1)

            dve.memset(mhalf[:], -0.5).then_inc(hid_ready, HID0)
            dve.memset(bn2[:], 0.0).then_inc(res_ready, HID0)
            dve.memset(bn6[:], 0.0).then_inc(hid_lo_ready, HID_LO0)
            dve.wait_ge(par_in, 16)
            softplus()
            for c in range(HEAD_CHUNKS):
                ada_copy(c)
                ada_sum(c)
            for s in range(RING):
                split_lo(s, s)
            norm(0)
            for l in range(DEPTH):
                up_stage(l, 0)
                down_stage(l, 0)
                norm(3 * l + 1)
                in_stage(l)
                out_stage(l)
                norm(3 * l + 2)
                up_stage(l, 1)
                down_stage(l, 1)
                norm(3 * l + 3)

        @block.gpsimd
        def _(pool):
            chain = [0]

            def link(ins):
                chain[0] += 1
                ins.then_inc(pool_chain, 1)
                pool.wait_ge(pool_chain, chain[0])

            def bias_of(l, m):
                c = C_BADA + (l * NMOD + m) * KD
                return par[:, c:c + KD].unsqueeze(2).to_broadcast([P, KD, 2])

            def prep_norm(l, i):
                n = 3 * l + i
                pool.wait_ge(mods_ready, l * LAYER_CHUNKS + 2 * (3 * i + 2))
                a, b = (l * NMOD + 3 * i) * KD, (l * NMOD + 3 * i + 1) * KD
                pool.tensor_tensor(n_shift[:, n, :, :], mods[:, a:a + KD, :], bias_of(l, 3 * i), ALU.add)
                link(pool.tensor_tensor(n_gain[:, n, :, :], mods[:, b:b + KD, :], bias_of(l, 3 * i + 1), ALU.add))
                link(pool.tensor_scalar(n_gain[:, n, :, :], n_gain[:, n, :, :], 1.0, None, ALU.add))
                g = C_GAIN + n * KD
                pool.tensor_tensor(n_gain[:, n, :, :], n_gain[:, n, :, :],
                                   par[:, g:g + KD].unsqueeze(2).to_broadcast([P, KD, 2]), ALU.mult).then_inc(prepped, 1)

            def prep_gate(l, i):
                n = 3 * l + i
                pool.wait_ge(mods_ready, l * LAYER_CHUNKS + 2 * (3 * i + 3))
                a = (l * NMOD + 3 * i + 2) * KD
                link(pool.tensor_tensor(gates[:, n, :, :], mods[:, a:a + KD, :], bias_of(l, 3 * i + 2), ALU.add))
                pool.tensor_scalar(gates[:, n, :, :], gates[:, n, :, :], 1.0 if i == 1 else 0.5, None,
                                   ALU.mult).then_inc(prepped, 1)

            def norm(n):
                w = dft(n)
                m4 = w // P
                for d in range(1, 7):
                    pool.wait_ge(sq_ready, KD * n + d + 1)
                    if d > 1:
                        pool.wait_ge(sqsum_ready, 6 * n + d - 1)
                    pool.tensor_tensor(scr[:, 2, 0:w], scr[:, 2, 0:w], scr[:, d % 2, 0:w], ALU.add).then_inc(sqsum_ready, 1)
                if n == 0:
                    prep_norm(0, 0)
                pool.wait_ge(var_ready, n + 1)
                pool.tensor_tensor(tokr[:, 0:m4], tok[:, 0:m4], mhalf[:, 0:m4], ALU.pow).then_inc(rstd_ready, 1)
                if n == 3 * DEPTH:
                    return
                for k in range(KD):
                    pool.wait_ge(z_hi_ready, KD * n + k + 1)
                    pool.tensor_tensor(z_lo[:, k, 0:w], scr[:, k % 3, 0:w], z_hi[:, k, 0:w].bitcast(F32),
                                       ALU.subtract).then_inc(z_ready, 1)

            def in_stage(l):
                wl = SEQ if l == DEPTH - 1 else T
                for u in range(8):
                    r = u % 4
                    pool.wait_ge(ti_ready, 8 * l + u + 1)
                    link(pool.tensor_scalar(l_bx[:, r, :], l_bx[:, r, :], 1.0, None, ALU.add))
                    pool.wait_ge(xc_ready, 4 * l + u // 2 + 1)
                    pool.tensor_tensor(l_bx[:, r, :], l_bx[:, r, :], xc[:, u // 2, :], ALU.mult).then_inc(bx_ready, 1)
                    if u == 3:
                        pool.wait_ge(vvar_ready, l + 1)
                        m4 = wl // P
                        link(pool.tensor_scalar(tok[:, 0:m4], bn2[:, 0:m4, 1], EPS, None, ALU.add))
                        pool.tensor_tensor(tokr[:, 0:m4], tok[:, 0:m4], mhalf[:, 0:m4], ALU.pow).then_inc(vrstd_ready, 1)
                for k in range(1, KD, 2):
                    pool.wait_ge(y_hi_ready, 8 * l + k + 1)
                    src = y_lru if k < 4 else y_sgu
                    pool.tensor_tensor(z_lo[:, k, 0:wl], src[:, k % 4, 0:wl], z_hi[:, k, 0:wl].bitcast(F32),
                                       ALU.subtract).then_inc(y_lo_pool, 1)

            def zero_blocks(l):
                pool.wait_ge(slot_done, AT[l, "in"]["slot"])
                pool.memset(xpad[:], 0.0)
                pool.memset(bd[:], 0.0).then_inc(bd_zero, 1)

            pool.memset(c_cols[:], 0.0)
            pool.memset(ones[:], 1.0)
            link(pool.memset(ident[:], 0.0))
            pool.affine_select(out=ident[:], in_=ident[:], compare_op=ALU.not_equal, fill=1.0, base=0,
                               pattern=[[-1, P]], channel_multiplier=1).then_inc(const_ready, 1)
            pool.wait_ge(par_in, 16)
            norm(0)
            for l in range(DEPTH):
                if l:
                    prep_norm(l, 2)
                    prep_gate(l, 2)
                else:
                    prep_gate(0, 0)
                    prep_norm(0, 1)
                norm(3 * l + 1)
                zero_blocks(l)
                if l == 0:
                    prep_gate(0, 1)
                    prep_norm(0, 2)
                in_stage(l)
                norm(3 * l + 2)
                if l == 0:
                    prep_gate(0, 2)
                    prep_norm(1, 0)
                    prep_gate(1, 0)
                    prep_norm(1, 1)
                    prep_gate(1, 1)
                norm(3 * l + 3)


def _weight_stream(w_in, w_out, w_in_mix, w_out_mix):
    parts = []

    def columns(w):
        n = w.shape[1] // P
        return w.reshape(KD, P, n, P).transpose(2, 1, 0, 3).reshape(n, P, SLOT)

    for f in range(2):
        up = w_in[f].reshape(KD, P, 2, KF, P).transpose(3, 2, 1, 0, 4).reshape(UP_SLOTS, P, SLOT)
        down = np.zeros((KD, P, 24, P), w_out[f].dtype)
        down[:, :, :KF] = w_out[f].reshape(KF, P, KD, P).transpose(2, 1, 0, 3)
        down = down.reshape(KD, P, 3, SLOT).transpose(0, 2, 1, 3).reshape(DOWN_SLOTS, P, SLOT)
        parts += [up, down]
        if f == 0:
            w = LT * P
            v = w_in_mix[:, 3 * w:].reshape(4, 2, P, w).transpose(0, 2, 1, 3).reshape(4, P, SLOT)
            parts += [columns(w_in_mix[:, :w]), v, columns(w_in_mix[:, w:2 * w]),
                      columns(w_in_mix[:, 2 * w:3 * w]), columns(w_out_mix)]
    return parts


def _columns(a):
    a = np.asarray(a)
    return a.reshape(-1, P).T


def kernel(**inputs):
    import concourse.bacc as bacc
    from concourse.bass_utils import run_bass_kernel_spmd

    t = {k: np.asarray(v) for k, v in inputs.items()}
    x_t = np.concatenate([t["x"][0], t["ctx"][0]], axis=0).T.reshape(KD, P, T).transpose(1, 0, 2)
    cvec = np.stack([t["c"][0].reshape(KD, P), t["c_ctx"].reshape(KD, P)], axis=1)
    gains = np.stack([t["ffn1_norm_g"], t["mix_norm_g"], t["ffn2_norm_g"]], axis=1)
    conv = np.concatenate([t["lru_conv_w"], t["lru_conv_b"][:, None]], axis=1)
    params = np.concatenate([_columns(a) for a in (
        cvec, t["b_ada"], gains, t["final_norm_g"], conv, t["lru_b_r"], t["lru_b_i"], t["lru_lambda"],
        t["sgu_norm_g"])], axis=1)
    assert params.shape == (P, N_PAR)
    ada_w = t["w_ada"].reshape(DEPTH, 2, 4, P, LAYER_CHUNKS, 2, 256).transpose(0, 4, 5, 1, 3, 2, 6)
    weights = np.concatenate([part for l in range(DEPTH) for part in _weight_stream(
        (t["ffn1_w_in"][l], t["ffn2_w_in"][l]), (t["ffn1_w_out"][l], t["ffn2_w_out"][l]),
        t["w_in_mix"][l], t["w_out_mix"][l])], axis=0)
    gate_w = np.stack([t["lru_w_r"], t["lru_w_i"]], axis=1).reshape(DEPTH, 2, 2, LT, 2, 64, 64)
    gate_w = gate_w.transpose(0, 4, 5, 1, 2, 3, 6).reshape(DEPTH, 2, 64, 16, 64)
    arrays = {
        "x_t": x_t, "params": params, "ada_w": ada_w.reshape(UNITS, P, SLOT), "weights": weights,
        "gate_w": gate_w, "sgu_w": t["sgu_w"].transpose(0, 3, 1, 2), "sgu_b": t["sgu_b"],
    }
    arrays = {k: np.ascontiguousarray(v) for k, v in arrays.items()}
    nc = bacc.Bacc("TRN2", target_bir_lowering=False, num_devices=1)
    args = [nc.dram_tensor(k, v.shape, F32, kind="ExternalInput").ap() for k, v in arrays.items()]
    out = nc.dram_tensor("out", (KD, P, SEQ), F32, kind="ExternalOutput").ap()
    build(nc, *args, out)
    got = run_bass_kernel_spmd(nc, [arrays], core_ids=[0]).results[0]["out"]
    return got.transpose(2, 0, 1).reshape(1, SEQ, D)
```

```python
from contextlib import ExitStack

import numpy as np
import concourse.bass as bass
from concourse import mybir

F32 = mybir.dt.float32
F32R = mybir.dt.float32r
ACT = mybir.ActivationFunctionType
ALU = mybir.AluOpType
AX_X = mybir.AxisListType.X

P = 128
D = 1024
KD = D // P
SEQ = 256
T = 512
DFF = 2816
KF = DFF // P
DEPTH = 2
LT = 4
NMOD = 9
EPS = 1e-6

RING = 4
SLOT = 8 * P
UP_SLOTS = 2 * KF
DOWN_SLOTS = 24
IN_SLOTS = 16
OUT_SLOTS = 8
LAYER_SLOTS = 2 * (UP_SLOTS + DOWN_SLOTS) + IN_SLOTS + OUT_SLOTS
SLOTS = DEPTH * LAYER_SLOTS

ADA_ORDER = [(0, 0), (0, 1), (0, 2), (0, 3), (0, 4), (0, 7), (0, 5), (0, 6), (0, 8), (1, 0), (1, 1),
             (1, 2), (1, 3), (1, 4), (1, 7), (1, 5), (1, 6), (1, 8)]
assert sorted(ADA_ORDER) == [(l, m) for l in range(DEPTH) for m in range(NMOD)]
HEAD_MODS = 2
RING_MODS = {(0, 0): 4, (0, 1): 1, (1, 0): 2, (1, 1): 0}
GAP_MODS = {1: 2, 2: 2, 3: 2, 4: 2, 5: 1}

Y_ORDER = (4, 0, 1, 5, 2, 3, 6, 7)
Y_POOL = 6
ADA_RING = 2

C_CVEC = 0
C_BADA = C_CVEC + KD * 2
C_GAIN = C_BADA + DEPTH * NMOD * KD
C_CONV = C_GAIN + (DEPTH * 3 + 1) * KD
C_BR = C_CONV + DEPTH * 5 * LT
C_BI = C_BR + DEPTH * 2 * LT
C_LAM = C_BI + DEPTH * 2 * LT
C_SGU = C_LAM + DEPTH * 2 * LT
N_PAR = C_SGU + DEPTH * LT


def schedule():
    at, slot, mod, ring, pre, ffn, tile = {}, 0, HEAD_MODS, 0, HEAD_MODS, 0, 0
    for l in range(DEPTH):
        for i, part in enumerate(("ffn0", "mix", "ffn1")):
            n = 3 * l + i
            at["norm", n] = dict(mod=mod, pre=pre, mods=GAP_MODS.get(n, 0))
            mod += GAP_MODS.get(n, 0)
            pre += GAP_MODS.get(n, 0)
            if part == "mix":
                at[l, "in"] = dict(slot=slot)
                slot += IN_SLOTS
                at[l, "out"] = dict(slot=slot, tile=tile)
                slot += OUT_SLOTS
            else:
                f = int(part[3])
                mods = RING_MODS[l, f]
                at[l, "up", f] = dict(slot=slot, mod=mod, ring=ring, ffn=ffn, mods=mods)
                slot += UP_SLOTS
                mod += mods
                ring += mods
                at[l, "down", f] = dict(slot=slot, ffn=ffn, tile=tile)
                slot += DOWN_SLOTS
                ffn += 1
            tile += KD
    at["norm", 3 * DEPTH] = dict(mods=0)
    assert slot == SLOTS and mod == len(ADA_ORDER)
    return at


AT = schedule()


def build(nc, x_t, params, ada_w, weights, gate_w, sgu_w, sgu_b, out):
    with ExitStack() as ctx:
        def sb(name, shape, dt=F32, scope=ctx):
            return scope.enter_context(nc.sbuf_tensor(name, shape, dt))

        def sem(name):
            return ctx.enter_context(nc.semaphore(name))

        res = sb("res", [P, KD, T])
        with ExitStack() as ada_scope:
            ada_z = sb("ada_z", [P, KD, SLOT], F32, ada_scope)
        z_hi = sb("z_hi", [P, KD, T], F32R)
        z_lo = sb("z_lo", [P, KD, T], F32R)
        raw = sb("raw", [P, RING, SLOT])
        w_hi = sb("w_hi", [P, RING, SLOT], F32R)
        w_lo = sb("w_lo", [P, RING, SLOT], F32R)
        ada_raw = sb("ada_raw", [P, ADA_RING, SLOT])
        ada_turned = sb("ada_turned", [P, KD, 32])
        scr = sb("scr", [P, 3, T])
        mods = sb("mods", [P, DEPTH * NMOD * KD, 2])
        n_gain = sb("n_gain", [P, DEPTH * 3, KD, 2])
        n_shift = sb("n_shift", [P, DEPTH * 3, KD, 2])
        gates = sb("gates", [P, DEPTH * 3, KD, 2])
        par = sb("par", [P, N_PAR])
        c_cols = sb("c_cols", [P, KD, 32])
        ident = sb("ident", [P, P])
        ones = sb("ones", [P, P])
        lam_t = sb("lam_t", [P, 6, DEPTH * 2 * LT])
        half_b = sb("half_b", [P, 2, DEPTH * 2 * LT])
        tok = sb("tok", [P, 4])
        tokr = sb("tokr", [P, 4])
        mhalf = sb("mhalf", [P, 4])
        bn6 = sb("bn6", [P, 4, 6])
        bn2 = sb("bn2", [P, 4, 2])

        with ExitStack() as ada_scope:
            ada_pre = sb("ada_pre", [P, 2 * KD, SLOT], F32, ada_scope)
        with ExitStack() as ffn_scope:
            h_hi = sb("h_hi", [P, KF, T], F32R, ffn_scope)
            h_lo = sb("h_lo", [P, KF, T], F32R, ffn_scope)
        with ExitStack() as y_scope:
            y_hi = sb("y_hi", [P, KD, T], F32R, y_scope)
            y_lo = sb("y_lo", [P, KD, T], F32R, y_scope)
        l_s = sb("l_s", [P, 4, T])
        l_q = sb("l_q", [P, 4, T])
        l_bx = sb("l_bx", [P, 4, T])
        l_a = sb("l_a", [P, 4, T])
        y_lru = sb("y_lru", [P, LT, T])
        gl = sb("gl", [P, LT, T])
        v_n = sb("v_n", [P, 4, 512])
        y_sgu = sb("y_sgu", [P, LT, T])
        xpad = sb("xpad", [P, 2, 2, SEQ + 3])
        xc = sb("xc", [P, LT, T])
        bd = sb("bd", [P, 16, P])
        ws = sb("ws", [P, LT, P])
        bs = sb("bs", [P, LT, P])

        bank = [ctx.enter_context(nc.psum_tensor(f"bank{i}", [P, 512], F32)) for i in range(8)]
        pa, po, p_ada, p_misc = bank[0:4], bank[4:6], bank[6], bank[7]

        raw_in = [sem(f"raw_in{i}") for i in range(RING)]
        ada_in = [sem(f"ada_in{i}") for i in range(ADA_RING)]
        hi_ready, lo_ready, slot_done = sem("hi_ready"), sem("lo_ready"), sem("slot_done")
        pre_in = [[sem(f"pre_in{m}_{i}") for i in range(4)] for m in range(2)]
        ada_used, pre_done = sem("ada_used"), sem("pre_done")
        turned, mods_ready = sem("turned"), sem("mods_ready")
        par_in, x_in, out_done, mix_in = sem("par_in"), sem("x_in"), sem("out_done"), sem("mix_in")
        const_ready, cvec_ready = sem("const_ready"), sem("cvec_ready")
        prepped, pool_chain, dve_chain, act_chain = sem("prepped"), sem("pool_chain"), sem("dve_chain"), sem("act_chain")
        silu_ready, hid_ready = sem("silu_ready"), sem("hid_ready")
        hid_hi_ready, hid_lo_ready = sem("hid_hi_ready"), sem("hid_lo_ready")
        res_ready, sq_ready, sqsum_ready = sem("res_ready"), sem("sq_ready"), sem("sqsum_ready")
        ss_done, var_ready, rstd_ready = sem("ss_done"), sem("var_ready"), sem("rstd_ready")
        diag_ready, bcast_done = sem("diag_ready"), sem("bcast_done")
        zt_ready, z_hi_ready, z_full_ready = sem("zt_ready"), sem("z_hi_ready"), sem("z_full_ready")
        z_ready = [sem("z_even_ready"), sem("z_odd_ready")]
        copy_ready, xc_ready, gate_mm = sem("copy_ready"), sem("xc_ready"), sem("gate_mm")
        ti_ready, exp_ready, bx_ready = sem("ti_ready"), sem("exp_ready"), sem("bx_ready")
        sqrt_ready, scan_ready = sem("sqrt_ready"), sem("scan_ready")
        gelu_ready, vvar_ready, vrstd_ready = sem("gelu_ready"), sem("vvar_ready"), sem("vrstd_ready")
        vn_ready, spatial_mm, zz_ready = sem("vn_ready"), sem("spatial_mm"), sem("zz_ready")
        y_ready, y_hi_ready = sem("y_ready"), sem("y_hi_ready")
        y_lo_dve, y_lo_pool = sem("y_lo_dve"), sem("y_lo_pool")
        lam_ready, bd_zero = sem("lam_ready"), sem("bd_zero")
        block = ctx.enter_context(nc.Block())

        HID0 = 2
        HID_LO0 = 1

        def dft(n):
            return SEQ if n >= 5 else T

        def streams(width):
            return 1 if width == SEQ else 2

        @block.sync
        def _(sp):
            def slot_dma(s, r):
                if isinstance(s, int) and s >= SLOTS:
                    return
                if not isinstance(s, int) or s >= RING:
                    sp.wait_ge(lo_ready, s - (RING - 1))
                src = weights[s] if isinstance(s, int) else weights[bass.ds(s, 1)].rearrange("a p n -> p (a n)")
                sp.dma_start(raw[:, r, :], src).then_inc(raw_in[r], 16)

            def unit_dma(at, i, p):
                if isinstance(i, int) and i == at["mods"] - 1 and p >= KD - ADA_RING:
                    nxt = [a for a in ring_stages if a["ring"] > at["ring"]]
                    if not nxt:
                        return
                    mod, p_ = nxt[0]["mod"], p - (KD - ADA_RING)
                else:
                    mod, p_ = at["mod"] + i, p + ADA_RING
                r = p % ADA_RING
                sp.wait_ge(ada_used, (at["ring"] + i) * KD + p + 1)
                u = mod * KD + p_
                src = ada_w[u] if isinstance(u, int) else ada_w[bass.ds(u, 1)].rearrange("a p n -> p (a n)")
                sp.dma_start(ada_raw[:, r, :], src).then_inc(ada_in[r], 16)

            def pre_dma(dst, mod, m, pairs=range(4)):
                for i in pairs:
                    u = mod * KD + 2 * i
                    sp.dma_start(dst[:, 2 * i:2 * i + 2, :],
                                 ada_w[u:u + 2].rearrange("a p n -> p a n")).then_inc(pre_in[m][i], 16)

            def stage(base):
                def body(i):
                    for q in range(4):
                        slot_dma(base + 8 + i * 4 + q, q)
                return body

            def ring_mod(at):
                def body(i):
                    for p in range(KD):
                        slot_dma(at["slot"] + 8 + i * KD + p, p % RING)
                        unit_dma(at, i, p)
                return body

            def run(body, n, peel):
                if n - peel > 0:
                    with sp.Fori(0, n - peel) as i:
                        body(i)
                for i in range(n - peel, n):
                    body(i)

            ring_stages = [AT[l, "up", f] for l in range(DEPTH) for f in range(2) if AT[l, "up", f]["mods"]]
            sp.dma_start(par[:], params).then_inc(par_in, 16)
            sp.dma_start(res[:], x_t).then_inc(x_in, 16)
            pre_dma(ada_pre[:, 0:KD], 0, 0)
            slot_dma(0, 0)
            pre_dma(ada_pre[:, KD:2 * KD], 1, 1)
            for s in range(1, RING):
                slot_dma(s, s)
            for r in range(ADA_RING):
                sp.dma_start(ada_raw[:, r, :], ada_w[HEAD_MODS * KD + r]).then_inc(ada_in[r], 16)
            for s in range(RING, 8):
                slot_dma(s, s % RING)
            for l in range(DEPTH):
                for f in range(2):
                    up, down = AT[l, "up", f], AT[l, "down", f]
                    if up["mods"]:
                        run(ring_mod(up), up["mods"], 1)
                    run(stage(up["slot"] + KD * up["mods"]), (UP_SLOTS - KD * up["mods"]) // 4, 0)
                    final = l == DEPTH - 1 and f == 1
                    if final:
                        run(stage(down["slot"]), DOWN_SLOTS // 4, 2)
                        continue
                    gap = AT["norm", 3 * l + 2 * f + 1]
                    body = stage(down["slot"])
                    for i in range(4):
                        body(i)
                        if i == 0:
                            sp.wait_ge(slot_done, down["slot"])
                        pre_dma(ada_z, gap["mod"], 1, (i,))
                    with sp.Fori(4, DOWN_SLOTS // 4) as i:
                        body(i)
                    sp.wait_ge(slot_done, down["slot"] + DOWN_SLOTS)
                    pre_dma(ada_pre[:, 0:KD], gap["mod"] + 1, 0)
                    if f == 0:
                        sp.wait_ge(bd_zero, l + 1)
                        for a in range(2):
                            sp.dma_start(bd[64 * a:64 * a + 64, :, 64 * a:64 * a + 64], gate_w[l, a]).then_inc(mix_in, 16)
                        sp.dma_start(ws[:], sgu_w[l]).then_inc(mix_in, 16)
                        sp.dma_start(bs[:], sgu_b[l].partition_broadcast(P)).then_inc(mix_in, 16)
                        body = stage(AT[l, "in"]["slot"])
                        gap = AT["norm", 3 * l + 2]
                        run(body, IN_SLOTS // 4, 0)
                        sp.wait_ge(slot_done, AT[l, "out"]["slot"])
                        for i in range(2):
                            pre_dma(ada_z, gap["mod"], 1, (2 * i, 2 * i + 1))
                            body(IN_SLOTS // 4 + i)
                        if gap["mods"] == 2:
                            sp.wait_ge(y_lo_dve, (KD - Y_POOL) * (l + 1))
                            sp.wait_ge(y_lo_pool, Y_POOL * (l + 1))
                            pre_dma(ada_pre[:, KD:2 * KD], gap["mod"] + 1, 0)
            for k in range(KD):
                sp.wait_ge(zt_ready, 6 * KD + k + 1)
                sp.dma_start(out[k], res[:, k, 0:SEQ]).then_inc(out_done, 16)
            sp.wait_ge(out_done, 16 * KD)

        @block.tensor
        def _(pe):
            def product(bank_ap, blk, r, rhs_hi, rhs_lo, start, stop):
                c = slice(blk * P, (blk + 1) * P)
                pe.matmul(bank_ap, w_hi[:, r, c], rhs_hi, start=start, stop=False)
                pe.matmul(bank_ap, w_hi[:, r, c], rhs_lo, start=False, stop=False)
                return pe.matmul(bank_ap, w_lo[:, r, c], rhs_hi, start=False, stop=stop)

            def ada_unit(dst, data, k):
                w = data.rearrange("p (b j i) -> p b j i", b=KD, j=4)
                for j in range(4):
                    m = pe.matmul(dst[32 * j:32 * j + 32, 0:256], c_cols[:, k, :], w[:, :, j, :],
                                  start=(k == 0), stop=(k == KD - 1), tile_position=(0, 32 * j))
                return m

            def ring_unit(at, i, p):
                if p == 0:
                    pe.wait_ge(mods_ready, at["mod"] - 1 if isinstance(i, int) and i == 0 else at["mod"] + i)
                pe.wait_ge(ada_in[p % 2], (at["ring"] * 4 + i * 4 + p // 2 + 1) * 16)
                ada_unit(p_ada, ada_raw[:, p % 2, :], p).then_inc(ada_used, 1)

            def pre_unit(mod, m, k, data, count):
                if k == 0 and mod >= HEAD_MODS:
                    pe.wait_ge(mods_ready, mod - 1 + m)
                if k % 2 == 0:
                    pe.wait_ge(pre_in[m][k // 2], 16 * count)
                mm = ada_unit((p_misc, p_ada)[m], data[:, k, :], k)
                if k == KD - 1:
                    mm.then_inc(pre_done, 1)

            def gap_unit(n, m, k):
                at = AT["norm", n]
                if at["mods"] >= 2 - m:
                    if m == 0:
                        data = ada_pre[:, KD:2 * KD] if n % 3 == 2 else ada_pre[:, 0:KD]
                    else:
                        data = ada_z
                    pre_unit(at["mod"] + 1 - m, m, k, data, n + 1)

            def norm(n):
                w = dft(n)
                if n == 0:
                    pe.wait_ge(const_ready, 1)
                for k in range(0, 2):
                    gap_unit(n, 1, k)
                pe.wait_ge(sqsum_ready, 6 * (n + 1))
                pe.wait_ge(res_ready, HID0 + KD * n)
                for src in (2, 1):
                    if src == 1:
                        pe.wait_ge(sq_ready, KD * (n + 1))
                    for m in range(w // P):
                        mm = pe.matmul(po[0][:, m:m + 1], scr[:, src, m * P:(m + 1) * P], ones[:, 0:1],
                                       start=(src == 2 and m == 0), stop=(src == 1), skip_group_check=True)
                mm.then_inc(ss_done, 1)
                for k in range(2, 5):
                    gap_unit(n, 1, k)
                pe.wait_ge(diag_ready, n + 1)
                pe.matmul(po[1][:, 0:w], ones[:], scr[:, 0, 0:w], start=True, stop=True).then_inc(bcast_done, 1)
                for k in range(5, KD):
                    gap_unit(n, 1, k)

            def up_stage(l, f):
                at = AT[l, "up", f]
                n = 3 * l + 2 * f
                w = dft(n)

                def slot(i, p, first=False):
                    q = p % 4
                    j2 = at["ffn"] * KF + i * 2 + p // 2
                    pe.wait_ge(lo_ready, at["slot"] + i * 4 + p + 1)
                    if q % 2 == 0:
                        pe.wait_ge(hid_ready, HID0 - 1 + j2)
                    for k in range(KD):
                        if first:
                            pe.wait_ge(z_ready[k % 2], KD // 2 * n + k // 2 + 1)
                        m = product(pa[q][:, 0:w], k, q, z_hi[:, k, 0:w], z_lo[:, k, 0:w], k == 0, k == KD - 1)
                        if k == KD - 1:
                            m.then_inc(slot_done, 1)
                        if first:
                            gap_unit(n, 0, k)

                for p in range(4):
                    slot(0, p, p == 0)
                    if at["mods"]:
                        ring_unit(at, 0, p)
                if at["mods"]:
                    for p in range(4, KD):
                        slot(0, p)
                        ring_unit(at, 0, p)
                if at["mods"] > 1:
                    with pe.Fori(1, at["mods"]) as i:
                        for p in range(KD):
                            slot(i * 2, p)
                            ring_unit(at, i, p)
                with pe.Fori(max(1, 2 * at["mods"]), UP_SLOTS // 4) as i:
                    for p in range(4):
                        slot(i, p)

            def down_stage(l, f):
                at = AT[l, "down", f]
                w = dft(3 * l + 2 * f)
                with pe.Fori(0, 2) as i:
                    for dd in range(4):
                        for part, n_blk in enumerate((8, 8, 6)):
                            q = 3 * dd + part
                            pe.wait_ge(lo_ready, at["slot"] + 1 + i * 12 + q)
                            if part == 0:
                                pe.wait_ge(res_ready, HID0 - 1 + at["tile"] + i * 4 + dd)
                            for b in range(n_blk):
                                k = 8 * part + b
                                if dd == 0 and k in (0, KF - 2, KF - 1):
                                    pe.wait_ge(hid_lo_ready, HID_LO0 + at["ffn"] * KF + max(k + 1, KF - 2))
                                m = product(po[dd % 2][:, 0:w], b, q % RING, h_hi[:, k, 0:w], h_lo[:, k, 0:w],
                                            k == 0, k == KF - 1)
                            m.then_inc(slot_done, 1)

            def in_stage(l):
                at = AT[l, "in"]
                n = 3 * l + 1
                wl = SEQ if l == DEPTH - 1 else T
                for q in range(IN_SLOTS):
                    pe.wait_ge(lo_ready, at["slot"] + q + 1)
                    kind, t = q // 4, q % 4
                    if kind in (0, 2):
                        if q == 1:
                            pe.wait_ge(zt_ready, KD * (n + 1))
                        elif q:
                            pe.wait_ge(copy_ready, 8 * l + (t - 1 if kind == 0 else t + 3))
                    if q == 4:
                        pe.wait_ge(hid_ready, HID0 + KF * (2 * l + 1))
                    if q == 12:
                        pe.wait_ge(vn_ready, l + 1)
                    w = T if kind == 0 else wl
                    if kind == 1:
                        for kk in range(2):
                            k = 2 * t + kk
                            c = slice(kk * 512, kk * 512 + 512)
                            for m_ in range(wl // P):
                                tk = slice(m_ * P, m_ * P + P)
                                pe.matmul(pa[m_][:], z_hi[:, k, tk], w_hi[:, q % 4, c], start=(k == 0), stop=False)
                                pe.matmul(pa[m_][:], z_lo[:, k, tk], w_hi[:, q % 4, c], start=False, stop=False)
                                m = pe.matmul(pa[m_][:], z_hi[:, k, tk], w_lo[:, q % 4, c], start=False, stop=(k == KD - 1))
                    else:
                        dst = pa[t] if kind == 3 else po[t % 2]
                        for k in range(KD):
                            if q == 0:
                                pe.wait_ge(z_ready[k % 2], KD // 2 * n + k // 2 + 1)
                            m = product(dst[:, 0:w], k, q % 4, z_hi[:, k, 0:w], z_lo[:, k, 0:w], k == 0, k == KD - 1)
                            if q == 0 and k < KD - 1:
                                gap_unit(n, 0, k)
                    m.then_inc(slot_done, 1)
                    if q == 0:
                        gap_unit(n, 0, KD - 1)
                    if 4 <= q < 12:
                        u = q - 4
                        t_, d_ = u // 2, u % 2
                        pe.wait_ge(xc_ready, 4 * l + t_ + 1)
                        if u == 0:
                            pe.wait_ge(mix_in, 64 * (l + 1))
                            pe.wait_ge(mods_ready, AT["norm", n]["mod"] + 2)
                        if u or l:
                            pe.wait_ge(ti_ready, 8 * l + u)
                        for kind_, dst in ((0, p_ada), (1, p_misc)):
                            m = pe.matmul(dst[:], bd[:, kind_ * 8 + d_ * 4 + t_, :], xc[:, t_, :], start=True, stop=True)
                        m.then_inc(gate_mm, 1)
                    if q >= 12:
                        g = q - 12
                        if g < 2:
                            pe.wait_ge(ti_ready, 8 * (l + 1))
                        else:
                            pe.wait_ge(zz_ready, 4 * l + g - 1)
                        dst = (p_ada, p_misc)[g % 2]
                        for m_ in range(wl // P):
                            m = pe.matmul(dst[:, m_ * P:(m_ + 1) * P], v_n[:, m_, g * P:(g + 1) * P], ws[:, g, :],
                                          start=True, stop=True)
                        m.then_inc(spatial_mm, 1)

            def out_stage(l):
                at = AT[l, "out"]
                w = SEQ if l == DEPTH - 1 else T
                def slot(i, q, first=False):
                    pe.wait_ge(lo_ready, at["slot"] + 1 + i * 4 + q)
                    pe.wait_ge(res_ready, HID0 - 1 + at["tile"] + i * 4 + q)
                    for n_, k in enumerate(Y_ORDER):
                        if first and n_ < Y_POOL:
                            pe.wait_ge(y_lo_pool, Y_POOL * l + n_ + 1)
                        elif first:
                            pe.wait_ge(y_lo_dve, (KD - Y_POOL) * l + n_ - Y_POOL + 1)
                        m = product(po[q % 2][:, 0:w], k, q, y_hi[:, k, 0:w], y_lo[:, k, 0:w], n_ == 0, n_ == KD - 1)
                    m.then_inc(slot_done, 1)

                pe.wait_ge(copy_ready, 8 * (l + 1))
                for q in range(4):
                    slot(0, q, q == 0)
                for q in range(4):
                    slot(1, q)

            pe.wait_ge(cvec_ready, 1)
            for k in range(KD):
                pre_unit(0, 0, k, ada_pre[:, 0:KD], 1)
            norm(0)
            for k in range(KD):
                pre_unit(1, 1, k, ada_pre[:, KD:2 * KD], 1)
            for l in range(DEPTH):
                up_stage(l, 0)
                down_stage(l, 0)
                norm(3 * l + 1)
                in_stage(l)
                out_stage(l)
                norm(3 * l + 2)
                up_stage(l, 1)
                down_stage(l, 1)
                norm(3 * l + 3)

        @block.scalar
        def _(act):
            def split_hi(s, r):
                if isinstance(s, int) and s >= SLOTS:
                    return
                if isinstance(s, int):
                    act.wait_ge(raw_in[r], 16 * (s // RING + 1))
                act.activation(w_hi[:, r, :], raw[:, r, :], ACT.Copy).then_inc(hi_ready, 1)

            def hi_in_loop(base, i, per, q):
                r = q % RING
                act.wait_ge(raw_in[r], 16 * ((base + q) // RING + 2) + i * (16 * per // RING))
                act.activation(w_hi[:, r, :], raw[:, r, :], ACT.Copy).then_inc(hi_ready, 1)

            def square(d, n):
                w = dft(n)
                if n:
                    act.wait_ge(res_ready, HID0 + KD * (n - 1) + d + 1)
                if d >= 3:
                    act.wait_ge(sqsum_ready, 6 * n + d - 2)
                dst = 2 if d == 0 else d % 2
                act.activation(scr[:, dst, 0:w], res[:, d, 0:w], ACT.Square).then_inc(sq_ready, 1)

            def norm(n):
                if n == 3 * DEPTH:
                    return
                w = dft(n)
                for k in range(KD):
                    act.wait_ge(zt_ready, KD * n + k + 1)
                    for s in range(streams(w)):
                        c = slice(s * SEQ, (s + 1) * SEQ)
                        m = act.activation(z_hi[:, k, c], scr[:, k % 3, c], ACT.Identity, bias=n_shift[:, n, k, s:s + 1])
                    m.then_inc(z_hi_ready, 1)
                    if k % 2:
                        act.wait_ge(z_hi_ready, KD * n + k + 1)
                        for s in range(streams(w)):
                            c = slice(s * SEQ, (s + 1) * SEQ)
                            m = act.activation(scr[:, k % 3, c], scr[:, k % 3, c], ACT.Identity,
                                               bias=n_shift[:, n, k, s:s + 1])
                        m.then_inc(z_full_ready, 1)

            def up_stage(l, f):
                at = AT[l, "up", f]
                w = dft(3 * l + 2 * f)
                with act.Fori(0, UP_SLOTS // 4) as i:
                    for q in range(4):
                        j = at["ffn"] * KF + i * 2 + q // 2
                        act.wait_ge(slot_done, at["slot"] + 1 + i * 4 + q)
                        if q % 2 == 0:
                            act.activation(scr[:, q // 2, 0:w], pa[q][:, 0:w], ACT.Silu).then_inc(silu_ready, 1)
                            hi_in_loop(at["slot"], i, 4, q)
                        else:
                            hi_in_loop(at["slot"], i, 4, q)
                            act.wait_ge(hid_ready, HID0 + 1 + j)
                            act.activation(h_hi[:, bass.ds(i * 2 + q // 2, 1), 0:w].rearrange("p a n -> p (a n)"),
                                           scr[:, 2, 0:w], ACT.Copy).then_inc(hid_hi_ready, 1)

            def down_stage(l, f):
                at = AT[l, "down", f]
                for q in range(DOWN_SLOTS):
                    act.wait_ge(slot_done, at["slot"] + q + 1)
                    split_hi(at["slot"] + q + 4, q % 4)
                    if q % 3 == 2:
                        square(q // 3, 3 * l + 2 * f + 1)

            def in_stage(l):
                at = AT[l, "in"]
                wl = SEQ if l == DEPTH - 1 else T
                ns = wl // SEQ
                for q in range(IN_SLOTS):
                    act.wait_ge(slot_done, at["slot"] + q + 1)
                    kind, t = q // 4, q % 4
                    if kind == 0:
                        if t >= 2:
                            act.wait_ge(xc_ready, 4 * l + t - 1)
                        elif t == 0:
                            act.wait_ge(bd_zero, l + 1)
                        act.activation(xpad[:, t % 2, :, 2:2 + SEQ], po[t % 2].rearrange("p (s n) -> p s n", s=2),
                                       ACT.Copy).then_inc(copy_ready, 1)
                    if kind == 2:
                        act.activation(gl[:, t, 0:wl], po[t % 2][:, 0:wl], ACT.Copy).then_inc(copy_ready, 1)
                    if 4 <= q < 12:
                        u = q - 4
                        t_, d_ = u // 2, u % 2
                        c = l * 8 + d_ * 4 + t_
                        r = u % 4
                        act.wait_ge(gate_mm, 8 * l + u + 1)
                        if u >= 4:
                            act.wait_ge(scan_ready, 4 * l + t_ - 1)
                        elif u == 0:
                            act.wait_ge(lam_ready, 3)
                        act.activation(l_q[:, r, :], p_ada[:], ACT.Tanh, bias=half_b[:, 0, c:c + 1], scale=0.5).then_inc(act_chain, 1)
                        act.activation(l_bx[:, r, :], p_misc[:], ACT.Tanh, bias=half_b[:, 1, c:c + 1], scale=0.5).then_inc(ti_ready, 1)
                        act.wait_ge(act_chain, 2 * (8 * l + u) + 1)
                        act.activation(l_s[:, r, :], l_q[:, r, :], ACT.Tanh, bias=lam_t[:, 4, c:c + 1],
                                       scale=lam_t[:, 4, c:c + 1]).then_inc(act_chain, 1)
                        act.activation(l_a[:, r, :], l_q[:, r, :], ACT.Exp, bias=lam_t[:, 5, c:c + 1],
                                       scale=lam_t[:, 5, c:c + 1]).then_inc(exp_ready, 1)
                        if d_ == 1:
                            for u_ in (u - 1, u):
                                act.wait_ge(act_chain, 2 * (8 * l + u_) + 2)
                                act.activation(l_s[:, u_ % 4, :], l_s[:, u_ % 4, :], ACT.Sqrt).then_inc(sqrt_ready, 1)
                    if q == 12:
                        for t_ in range(LT):
                            act.wait_ge(copy_ready, 8 * (l + 1))
                            act.activation(gl[:, t_, 0:wl], gl[:, t_, 0:wl], ACT.Gelu_apprx_tanh).then_inc(gelu_ready, 1)
                for n_, k in enumerate(Y_ORDER):
                    act.wait_ge(y_ready, 8 * l + n_ + 1)
                    src = y_lru if k < 4 else y_sgu
                    act.activation(y_hi[:, k, 0:wl], src[:, k % 4, 0:wl], ACT.Copy).then_inc(y_hi_ready, 1)

            def out_stage(l):
                at = AT[l, "out"]
                act.wait_ge(hi_ready, at["slot"] + 4)
                for q in range(OUT_SLOTS):
                    act.wait_ge(slot_done, at["slot"] + q + 1)
                    split_hi(at["slot"] + q + 4, q % 4)
                    square(q, 3 * l + 2)

            act.wait_ge(par_in, 16)
            act.wait_ge(const_ready, 1)
            act.activation(c_cols[:, :, 0:2], par[:, C_CVEC:C_CVEC + 2 * KD].rearrange("p (k s) -> p k s", s=2),
                           ACT.Silu).then_inc(cvec_ready, 1)
            act.wait_ge(lam_ready, 1)
            act.activation(lam_t[:, 1, :], lam_t[:, 0, :], ACT.Exp, scale=-1.0).then_inc(lam_ready, 1)
            act.wait_ge(x_in, 16)
            for d in range(KD):
                square(d, 0)
            for s in range(RING):
                split_hi(s, s)
            norm(0)
            for l in range(DEPTH):
                up_stage(l, 0)
                down_stage(l, 0)
                norm(3 * l + 1)
                in_stage(l)
                out_stage(l)
                norm(3 * l + 2)
                up_stage(l, 1)
                down_stage(l, 1)
                norm(3 * l + 3)

        @block.vector
        def _(dve):
            chain = [0]

            def link(ins):
                chain[0] += 1
                ins.then_inc(dve_chain, 1)
                dve.wait_ge(dve_chain, chain[0])

            def split_lo(s, r):
                if isinstance(s, int) and s >= SLOTS:
                    return
                dve.wait_ge(hi_ready, s + 1)
                dve.tensor_tensor(w_lo[:, r, :], raw[:, r, :], w_hi[:, r, :].bitcast(F32), ALU.subtract).then_inc(lo_ready, 1)

            def ada_turn(mod, m):
                if not isinstance(mod, int) or mod:
                    dve.wait_ge(mods_ready, mod)
                dve.transpose(ada_turned.rearrange("p b r -> p (b r)"), (p_misc, p_ada)[m][:, 0:256]).then_inc(turned, 1)
                dve.wait_ge(turned, mod + 1)
                dst = mods[:, mod * KD:mod * KD + KD, :] if isinstance(mod, int) else mods[:, bass.ds(mod * KD, KD), :]
                dve.tensor_copy(dst, ada_turned[:, :, 0:2]).then_inc(mods_ready, 1)

            def pre_turn(n, m):
                at = AT["norm", n]
                if at["mods"] >= 2 - m:
                    dve.wait_ge(pre_done, at["pre"] + 2 - m)
                    ada_turn(at["mod"] + 1 - m, m)

            def residual(l, norm_i, d, w, tile):
                if d == 0:
                    dve.wait_ge(prepped, 6 * l + 2 * norm_i + 2)
                for s in range(streams(w)):
                    c = slice(s * SEQ, (s + 1) * SEQ)
                    m = dve.scalar_tensor_tensor(res[:, d, c], po[d % 2][:, c], gates[:, 3 * l + norm_i, d, s:s + 1],
                                                 res[:, d, c], ALU.mult, ALU.add)
                m.then_inc(res_ready, 1)

            def norm(n):
                w = dft(n)
                m4 = w // P
                dve.wait_ge(ss_done, n + 1)
                dve.tensor_scalar(tok[:, 0:m4], po[0][:, 0:m4], 1.0 / D, EPS, ALU.mult, ALU.add).then_inc(var_ready, 1)
                dve.wait_ge(rstd_ready, n + 1)
                dve.tensor_tensor(scr[:, 0, 0:w].rearrange("p (m j) -> p m j", j=P),
                                  ident[:].unsqueeze(1).to_broadcast([P, m4, P]),
                                  tokr[:, 0:m4].unsqueeze(2).to_broadcast([P, m4, P]), ALU.mult).then_inc(diag_ready, 1)
                dve.wait_ge(bcast_done, n + 1)
                if n == 0:
                    dve.wait_ge(pre_done, 2)
                    ada_turn(1, 1)
                if n < 3 * DEPTH:
                    dve.wait_ge(prepped, 2 * n + 1)
                if n == 3 * DEPTH:
                    for k in range(KD):
                        if k >= 3:
                            dve.wait_ge(zt_ready, KD * n + k - 2)
                        link(dve.tensor_tensor(scr[:, k % 3, 0:w], res[:, k, 0:w], po[1][:, 0:w], ALU.mult))
                        g = C_GAIN + n * KD + k
                        dve.tensor_scalar(res[:, k, 0:w], scr[:, k % 3, 0:w], par[:, g:g + 1], None, ALU.mult).then_inc(zt_ready, 1)
                    return

                def scaled(k):
                    if k >= 3:
                        dve.wait_ge(z_ready[(k - 3) % 2], KD // 2 * n + (k - 3) // 2 + 1)
                    for s in range(streams(w)):
                        c = slice(s * SEQ, (s + 1) * SEQ)
                        m = dve.scalar_tensor_tensor(scr[:, k % 3, c], res[:, k, c], n_gain[:, n, k, s:s + 1],
                                                     po[1][:, c], ALU.mult, ALU.mult)
                    m.then_inc(zt_ready, 1)

                def z_low(k):
                    dve.wait_ge(z_hi_ready, KD * n + k + 1)
                    for s in range(streams(w)):
                        c = slice(s * SEQ, (s + 1) * SEQ)
                        m = dve.scalar_tensor_tensor(z_lo[:, k, c], scr[:, k % 3, c], n_shift[:, n, k, s:s + 1],
                                                     z_hi[:, k, c].bitcast(F32), ALU.add, ALU.subtract)
                    m.then_inc(z_ready[0], 1)

                scaled(0)
                for k in range(0, KD, 2):
                    scaled(k + 1)
                    if n and k == 0:
                        dve.wait_ge(pre_done, AT["norm", n]["pre"] + 1)
                    z_low(k)
                    if k + 2 < KD:
                        scaled(k + 2)
                    if n == 0 and k == 4:
                        split_lo(1, 1)
                pre_turn(n, 1)

            def up_stage(l, f):
                at = AT[l, "up", f]
                w = dft(3 * l + 2 * f)

                def slot(i, p):
                    q = p % 4
                    s = at["slot"] + i * 4 + p
                    dve.wait_ge(slot_done, s + 1)
                    if q % 2 == 1:
                        jj = i * 2 + p // 2
                        j = at["ffn"] * KF + jj
                        dve.wait_ge(silu_ready, j + 1)
                        dve.wait_ge(hid_lo_ready, HID_LO0 + j)
                        dve.tensor_tensor(scr[:, 2, 0:w], scr[:, q // 2, 0:w], pa[q][:, 0:w], ALU.mult).then_inc(hid_ready, 1)
                    split_lo(s + 4, q)
                    if q % 2 == 1:
                        dve.wait_ge(hid_hi_ready, j + 1)
                        hid = slice(jj, jj + 1) if isinstance(jj, int) else bass.ds(jj, 1)
                        dve.tensor_tensor(h_lo[:, hid, 0:w].rearrange("p a n -> p (a n)"), scr[:, 2, 0:w],
                                          h_hi[:, hid, 0:w].rearrange("p a n -> p (a n)").bitcast(F32),
                                          ALU.subtract).then_inc(hid_lo_ready, 1)

                def ring_mod(i, first=False):
                    for p in range(KD):
                        slot(i * 2, p)
                        if first and p == 0:
                            pre_turn(3 * l + 2 * f, 0)
                    dve.wait_ge(ada_used, (at["ring"] + i + 1) * KD)
                    ada_turn(at["mod"] + i, 1)

                if at["mods"]:
                    ring_mod(0, True)
                else:
                    for p in range(4):
                        slot(0, p)
                        if p == 0:
                            pre_turn(3 * l + 2 * f, 0)
                if at["mods"] > 1:
                    with dve.Fori(1, at["mods"]) as i:
                        ring_mod(i)
                with dve.Fori(max(1, 2 * at["mods"]), UP_SLOTS // 4) as i:
                    for p in range(4):
                        slot(i, p)

            def down_stage(l, f):
                at = AT[l, "down", f]
                w = dft(3 * l + 2 * f)
                for q in range(DOWN_SLOTS):
                    dve.wait_ge(slot_done, at["slot"] + q + 1)
                    if q % 3 == 2:
                        residual(l, 2 * f, q // 3, w, at["tile"])
                    split_lo(at["slot"] + q + 4, q % 4)

            def conv(l, t):
                dve.wait_ge(copy_ready, 8 * l + t + 1)
                o = xc[:, t, :].rearrange("p (s n) -> p s n", s=2)
                c = C_CONV + l * 5 * LT + t
                link(dve.tensor_scalar(o, xpad[:, t % 2, :, 0:SEQ], par[:, c:c + 1], par[:, c + 4 * LT:c + 4 * LT + 1],
                                       ALU.mult, ALU.add))
                for k in range(1, 4):
                    m = dve.scalar_tensor_tensor(o, xpad[:, t % 2, :, k:k + SEQ], par[:, c + k * LT:c + k * LT + 1], o,
                                                 ALU.mult, ALU.add)
                    if k < 3:
                        link(m)
                m.then_inc(xc_ready, 1)

            def scans(l, t):
                for d in range(2):
                    u = 2 * t + d
                    r = u % 4
                    dve.wait_ge(exp_ready, 8 * l + u + 1)
                    dve.wait_ge(bx_ready, 8 * l + u + 1)
                    link(dve.scalar_tensor_tensor(l_q[:, r, :], l_a[:, r, :], 1.0, l_bx[:, r, :], ALU.add, ALU.mult))
                    dve.wait_ge(sqrt_ready, 8 * l + u + 1)
                    link(dve.scalar_tensor_tensor(l_q[:, r, :], l_q[:, r, :], 0.5, l_s[:, r, :], ALU.mult, ALU.mult))
                    if d == 0:
                        link(dve.tensor_tensor_scan(l_bx[:, r, SEQ:T], l_a[:, r, SEQ:T], l_q[:, r, SEQ:T], 0.0,
                                                    ALU.mult, ALU.add))
                        dve.tensor_tensor_scan(l_bx[:, r, 0:SEQ], l_a[:, r, 0:SEQ], l_q[:, r, 0:SEQ],
                                               l_bx[:, r, T - 1:T], ALU.mult, ALU.add)
                    else:
                        link(dve.tensor_tensor_scan(l_bx[:, r, ::-1], l_a[:, r, ::-1], l_q[:, r, ::-1], 0.0,
                                                    ALU.mult, ALU.add))
                r0 = (2 * t) % 4
                dve.tensor_tensor(y_lru[:, t, :], l_bx[:, r0, :], l_bx[:, r0 + 1, :], ALU.add).then_inc(scan_ready, 1)

            def in_stage(l):
                at = AT[l, "in"]
                wl = SEQ if l == DEPTH - 1 else T
                m4 = wl // P
                for q in range(IN_SLOTS):
                    dve.wait_ge(slot_done, at["slot"] + q + 1)
                    s = at["slot"] + q + 4
                    dve.wait_ge(raw_in[q % 4], 16 * (s // RING + 1))
                    dve.tensor_copy(w_hi[:, q % 4, :], raw[:, q % 4, :]).then_inc(hi_ready, 1)
                    if q < 4:
                        conv(l, q)
                    split_lo(s, q % 4)
                    if q == 0:
                        pre_turn(3 * l + 1, 0)
                    if q == 7:
                        for m_ in range(m4):
                            m = dve.bn_stats(bn6[:, m_, :], pa[m_][:])
                        link(m)
                        for m_ in range(m4):
                            m = dve.bn_aggr(bn2[:, m_, :], bn6[:, m_, :])
                        m.then_inc(vvar_ready, 1)
                    if q == 9:
                        dve.wait_ge(vrstd_ready, l + 1)
                        for m_ in range(m4):
                            m = dve.tensor_scalar(v_n[:, m_, :], pa[m_][:], bn2[:, m_, 0:1], tokr[:, m_:m_ + 1],
                                                  ALU.subtract, ALU.mult)
                        m.then_inc(vn_ready, 1)
                    if q in (6, 8, 10, 12):
                        scans(l, (q - 6) // 2)
                    if q >= 12:
                        g = q - 12
                        dve.wait_ge(spatial_mm, 4 * l + g + 1)
                        src = (p_ada, p_misc)[g % 2][:, 0:wl].rearrange("p (m j) -> p m j", j=P)
                        o = y_sgu[:, g, 0:wl].rearrange("p (m j) -> p m j", j=P)
                        c = C_SGU + l * LT + g
                        if g == 0:
                            dve.wait_ge(mix_in, 64 * (l + 1))
                        dve.scalar_tensor_tensor(o, src, par[:, c:c + 1], bs[:, g, :].unsqueeze(1).to_broadcast([P, m4, P]),
                                                 ALU.mult, ALU.add).then_inc(zz_ready, 1)
                        for n_ in {0: (), 1: (0, 1, 2), 2: (3, 4, 5), 3: (6, 7)}[g]:
                            k = Y_ORDER[n_]
                            if k < 4:
                                dve.wait_ge(gelu_ready, 4 * l + k + 1)
                                dve.wait_ge(scan_ready, 4 * l + k + 1)
                                y, factor = y_lru, gl[:, k, 0:wl]
                            else:
                                dve.wait_ge(zz_ready, 4 * l + k - 3)
                                y, factor = y_sgu, pa[k - 4][:, 0:wl]
                            dve.tensor_tensor(y[:, k % 4, 0:wl], y[:, k % 4, 0:wl], factor, ALU.mult).then_inc(y_ready, 1)
                for n_ in range(Y_POOL, KD):
                    k = Y_ORDER[n_]
                    src = y_lru if k < 4 else y_sgu
                    dve.wait_ge(y_hi_ready, 8 * l + n_ + 1)
                    dve.tensor_tensor(y_lo[:, k, 0:wl], src[:, k % 4, 0:wl], y_hi[:, k, 0:wl].bitcast(F32),
                                      ALU.subtract).then_inc(y_lo_dve, 1)

            def out_stage(l):
                at = AT[l, "out"]
                w = SEQ if l == DEPTH - 1 else T
                for q in range(OUT_SLOTS):
                    dve.wait_ge(slot_done, at["slot"] + q + 1)
                    residual(l, 1, q, w, at["tile"])
                    split_lo(at["slot"] + q + 4, q % 4)

            def softplus():
                lam = par[:, C_LAM:C_LAM + DEPTH * 2 * LT]
                link(dve.tensor_scalar(lam_t[:, 0, :], lam, -1.0, None, ALU.mult))
                dve.tensor_tensor(lam_t[:, 0, :], lam_t[:, 0, :], lam, ALU.max).then_inc(lam_ready, 1)
                dve.wait_ge(lam_ready, 2)
                link(dve.tensor_scalar(lam_t[:, 2, :], lam_t[:, 1, :], 2.0, None, ALU.add))
                link(dve.reciprocal(lam_t[:, 2, :], lam_t[:, 2, :]))
                link(dve.tensor_tensor(lam_t[:, 1, :], lam_t[:, 1, :], lam_t[:, 2, :], ALU.mult))
                link(dve.tensor_tensor(lam_t[:, 2, :], lam_t[:, 1, :], lam_t[:, 1, :], ALU.mult))
                link(dve.tensor_scalar(lam_t[:, 3, :], lam_t[:, 2, :], 1.0 / 17, None, ALU.mult))
                for c in range(15, 1, -2):
                    link(dve.scalar_tensor_tensor(lam_t[:, 3, :], lam_t[:, 3, :], 1.0 / c, lam_t[:, 2, :], ALU.add, ALU.mult))
                link(dve.scalar_tensor_tensor(lam_t[:, 3, :], lam_t[:, 3, :], 1.0, lam_t[:, 1, :], ALU.add, ALU.mult))
                link(dve.tensor_scalar(lam_t[:, 0, :], lam, -1.0, 0.0, ALU.mult, ALU.max))
                link(dve.scalar_tensor_tensor(lam_t[:, 3, :], lam_t[:, 3, :], 2.0, lam_t[:, 0, :], ALU.mult, ALU.add))
                dve.tensor_scalar(lam_t[:, 4, :], lam_t[:, 3, :], 2.0, None, ALU.mult)
                dve.tensor_scalar(lam_t[:, 5, :], lam_t[:, 3, :], -4.0, None, ALU.mult)
                dve.tensor_scalar(half_b[:, 0, :], par[:, C_BR:C_BR + DEPTH * 2 * LT], 0.5, None, ALU.mult)
                dve.tensor_scalar(half_b[:, 1, :], par[:, C_BI:C_BI + DEPTH * 2 * LT], 0.5, None, ALU.mult).then_inc(lam_ready, 1)

            dve.memset(mhalf[:], -0.5).then_inc(hid_ready, HID0)
            dve.memset(bn2[:], 0.0).then_inc(res_ready, HID0)
            dve.memset(bn6[:], 0.0).then_inc(hid_lo_ready, HID_LO0)
            dve.wait_ge(par_in, 16)
            softplus()
            dve.wait_ge(pre_done, 1)
            ada_turn(0, 0)
            split_lo(0, 0)
            norm(0)
            for s in range(2, RING):
                split_lo(s, s)
            for l in range(DEPTH):
                up_stage(l, 0)
                down_stage(l, 0)
                norm(3 * l + 1)
                in_stage(l)
                out_stage(l)
                norm(3 * l + 2)
                up_stage(l, 1)
                down_stage(l, 1)
                norm(3 * l + 3)

        @block.gpsimd
        def _(pool):
            chain = [0]

            def link(ins):
                chain[0] += 1
                ins.then_inc(pool_chain, 1)
                pool.wait_ge(pool_chain, chain[0])

            def bias_of(l, m):
                c = C_BADA + (l * NMOD + m) * KD
                return par[:, c:c + KD].unsqueeze(2).to_broadcast([P, KD, 2])

            def prep_norm(l, i):
                n = 3 * l + i
                at = [ADA_ORDER.index((l, 3 * i + j)) for j in range(2)]
                pool.wait_ge(mods_ready, max(at) + 1)
                a, b = at[0] * KD, at[1] * KD
                pool.tensor_tensor(n_shift[:, n, :, :], mods[:, a:a + KD, :], bias_of(l, 3 * i), ALU.add)
                link(pool.tensor_tensor(n_gain[:, n, :, :], mods[:, b:b + KD, :], bias_of(l, 3 * i + 1), ALU.add))
                link(pool.tensor_scalar(n_gain[:, n, :, :], n_gain[:, n, :, :], 1.0, None, ALU.add))
                g = C_GAIN + n * KD
                pool.tensor_tensor(n_gain[:, n, :, :], n_gain[:, n, :, :],
                                   par[:, g:g + KD].unsqueeze(2).to_broadcast([P, KD, 2]), ALU.mult).then_inc(prepped, 1)

            def prep_gate(l, i):
                n = 3 * l + i
                at = ADA_ORDER.index((l, 3 * i + 2))
                pool.wait_ge(mods_ready, at + 1)
                a = at * KD
                link(pool.tensor_tensor(gates[:, n, :, :], mods[:, a:a + KD, :], bias_of(l, 3 * i + 2), ALU.add))
                pool.tensor_scalar(gates[:, n, :, :], gates[:, n, :, :], 1.0 if i == 1 else 0.5, None,
                                   ALU.mult).then_inc(prepped, 1)

            def norm(n):
                w = dft(n)
                m4 = w // P
                for d in range(1, 7):
                    pool.wait_ge(sq_ready, KD * n + d + 1)
                    if d > 1:
                        pool.wait_ge(sqsum_ready, 6 * n + d - 1)
                    pool.tensor_tensor(scr[:, 2, 0:w], scr[:, 2, 0:w], scr[:, d % 2, 0:w], ALU.add).then_inc(sqsum_ready, 1)
                pool.wait_ge(var_ready, n + 1)
                pool.tensor_tensor(tokr[:, 0:m4], tok[:, 0:m4], mhalf[:, 0:m4], ALU.pow).then_inc(rstd_ready, 1)
                if n == 0:
                    prep_norm(0, 0)
                if n == 3 * DEPTH:
                    return
                if n:
                    pool.wait_ge(pre_done, AT["norm", n]["pre"] + 1)
                for k in range(1, KD, 2):
                    pool.wait_ge(z_full_ready, KD // 2 * n + k // 2 + 1)
                    pool.tensor_tensor(z_lo[:, k, 0:w], scr[:, k % 3, 0:w], z_hi[:, k, 0:w].bitcast(F32),
                                       ALU.subtract).then_inc(z_ready[1], 1)

            def in_stage(l):
                wl = SEQ if l == DEPTH - 1 else T
                for u in range(8):
                    r = u % 4
                    pool.wait_ge(ti_ready, 8 * l + u + 1)
                    pool.wait_ge(xc_ready, 4 * l + u // 2 + 1)
                    link(pool.tensor_tensor(l_bx[:, r, :], l_bx[:, r, :], xc[:, u // 2, :], ALU.mult))
                    pool.tensor_tensor(l_bx[:, r, :], l_bx[:, r, :], xc[:, u // 2, :], ALU.add).then_inc(bx_ready, 1)
                    if u == 3:
                        pool.wait_ge(vvar_ready, l + 1)
                        m4 = wl // P
                        link(pool.tensor_scalar(tok[:, 0:m4], bn2[:, 0:m4, 1], EPS, None, ALU.add))
                        pool.tensor_tensor(tokr[:, 0:m4], tok[:, 0:m4], mhalf[:, 0:m4], ALU.pow).then_inc(vrstd_ready, 1)
                for n_ in range(Y_POOL):
                    k = Y_ORDER[n_]
                    pool.wait_ge(y_hi_ready, 8 * l + n_ + 1)
                    src = y_lru if k < 4 else y_sgu
                    pool.tensor_tensor(y_lo[:, k, 0:wl], src[:, k % 4, 0:wl], y_hi[:, k, 0:wl].bitcast(F32),
                                       ALU.subtract).then_inc(y_lo_pool, 1)

            def zero_blocks(l):
                pool.wait_ge(slot_done, AT[l, "in"]["slot"])
                pool.memset(xpad[:], 0.0)
                pool.memset(bd[:], 0.0).then_inc(bd_zero, 1)

            pool.memset(c_cols[:], 0.0)
            pool.memset(ones[:], 1.0)
            link(pool.memset(ident[:], 0.0))
            pool.affine_select(out=ident[:], in_=ident[:], compare_op=ALU.not_equal, fill=1.0, base=0,
                               pattern=[[-1, P]], channel_multiplier=1).then_inc(const_ready, 1)
            pool.wait_ge(par_in, 16)
            norm(0)
            for l in range(DEPTH):
                prep_gate(l, 0)
                prep_norm(l, 1)
                norm(3 * l + 1)
                zero_blocks(l)
                prep_gate(l, 1)
                prep_norm(l, 2)
                in_stage(l)
                norm(3 * l + 2)
                prep_gate(l, 2)
                if l == 0:
                    prep_norm(1, 0)
                norm(3 * l + 3)


def _weight_stream(w_in, w_out, w_in_mix, w_out_mix):
    parts = []

    def columns(w):
        n = w.shape[1] // P
        return w.reshape(KD, P, n, P).transpose(2, 1, 0, 3).reshape(n, P, SLOT)

    for f in range(2):
        up = w_in[f].reshape(KD, P, 2, KF, P).transpose(3, 2, 1, 0, 4).reshape(UP_SLOTS, P, SLOT)
        down = np.zeros((KD, P, 24, P), w_out[f].dtype)
        down[:, :, :KF] = w_out[f].reshape(KF, P, KD, P).transpose(2, 1, 0, 3)
        down = down.reshape(KD, P, 3, SLOT).transpose(0, 2, 1, 3).reshape(DOWN_SLOTS, P, SLOT)
        parts += [up, down]
        if f == 0:
            w = LT * P
            v = w_in_mix[:, 3 * w:].reshape(4, 2, P, w).transpose(0, 2, 1, 3).reshape(4, P, SLOT)
            parts += [columns(w_in_mix[:, :w]), v, columns(w_in_mix[:, w:2 * w]),
                      columns(w_in_mix[:, 2 * w:3 * w]), columns(w_out_mix)]
    return parts


def _columns(a):
    a = np.asarray(a)
    return a.reshape(-1, P).T


def kernel(**inputs):
    import concourse.bacc as bacc
    from concourse.bass_utils import run_bass_kernel_spmd

    t = {k: np.asarray(v) for k, v in inputs.items()}
    x_t = np.concatenate([t["x"][0], t["ctx"][0]], axis=0).T.reshape(KD, P, T).transpose(1, 0, 2)
    cvec = np.stack([t["c"][0].reshape(KD, P), t["c_ctx"].reshape(KD, P)], axis=1)
    gains = np.stack([t["ffn1_norm_g"], t["mix_norm_g"], t["ffn2_norm_g"]], axis=1)
    conv = np.concatenate([t["lru_conv_w"], t["lru_conv_b"][:, None]], axis=1)
    params = np.concatenate([_columns(a) for a in (
        cvec, t["b_ada"], gains, t["final_norm_g"], conv, t["lru_b_r"], t["lru_b_i"], t["lru_lambda"],
        t["sgu_norm_g"])], axis=1)
    assert params.shape == (P, N_PAR)
    ada_w = np.stack([t["w_ada"][l, :, m * D:(m + 1) * D] for l, m in ADA_ORDER])
    weights = np.concatenate([part for l in range(DEPTH) for part in _weight_stream(
        (t["ffn1_w_in"][l], t["ffn2_w_in"][l]), (t["ffn1_w_out"][l], t["ffn2_w_out"][l]),
        t["w_in_mix"][l], t["w_out_mix"][l])], axis=0)
    gate_w = np.stack([t["lru_w_r"], t["lru_w_i"]], axis=1).reshape(DEPTH, 2, 2, LT, 2, 64, 64)
    gate_w = gate_w.transpose(0, 4, 5, 1, 2, 3, 6).reshape(DEPTH, 2, 64, 16, 64)
    arrays = {
        "x_t": x_t, "params": params, "ada_w": ada_w.reshape(len(ADA_ORDER) * KD, P, D), "weights": weights,
        "gate_w": gate_w, "sgu_w": t["sgu_w"].transpose(0, 3, 1, 2), "sgu_b": t["sgu_b"],
    }
    arrays = {k: np.ascontiguousarray(v) for k, v in arrays.items()}
    nc = bacc.Bacc("TRN2", target_bir_lowering=False, num_devices=1)
    args = [nc.dram_tensor(k, v.shape, F32, kind="ExternalInput").ap() for k, v in arrays.items()]
    out = nc.dram_tensor("out", (KD, P, SEQ), F32, kind="ExternalOutput").ap()
    build(nc, *args, out)
    got = run_bass_kernel_spmd(nc, [arrays], core_ids=[0]).results[0]["out"]
    return got.transpose(2, 0, 1).reshape(1, SEQ, D)
```

```python
from contextlib import ExitStack

import numpy as np
import concourse.bass as bass
from concourse import mybir

F32 = mybir.dt.float32
F32R = mybir.dt.float32r
ACT = mybir.ActivationFunctionType
ALU = mybir.AluOpType
AX_X = mybir.AxisListType.X

P = 128
D = 1024
KD = D // P
SEQ = 256
T = 512
DFF = 2816
KF = DFF // P
DEPTH = 2
LT = 4
NMOD = 9
EPS = 1e-6

RING = 4
SLOT = 8 * P
UP_SLOTS = 2 * KF
DOWN_SLOTS = 24
IN_SLOTS = 16
OUT_SLOTS = 8
LAYER_SLOTS = 2 * (UP_SLOTS + DOWN_SLOTS) + IN_SLOTS + OUT_SLOTS
SLOTS = DEPTH * LAYER_SLOTS

ADA_ORDER = [(0, 2), (0, 3), (0, 4), (0, 6), (0, 7), (0, 5), (0, 8), (1, 0), (1, 1), (1, 3),
             (1, 2), (1, 4), (1, 6), (1, 7), (1, 5), (1, 8)]
assert sorted(ADA_ORDER) == [(l, m) for l in range(DEPTH) for m in range(NMOD)][2:]
RING_MODS = {(0, 0): 5, (0, 1): 3, (1, 0): 3, (1, 1): 0}

Y_ORDER = (4, 0, 1, 5, 2, 3, 6, 7)
Y_POOL = 6
SIDE = 2
HEAD_SIDE = 4
MIX_HI_DVE = range(4, 16)
HALF = D // 2
ADA_RING = 2

C_CVEC = 0
C_BADA = C_CVEC + KD * 2
C_GAIN = C_BADA + DEPTH * NMOD * KD
C_CONV = C_GAIN + (DEPTH * 3 + 1) * KD
C_BR = C_CONV + DEPTH * 5 * LT
C_BI = C_BR + DEPTH * 2 * LT
C_LAM = C_BI + DEPTH * 2 * LT
C_SGU = C_LAM + DEPTH * 2 * LT
N_PAR = C_SGU + DEPTH * LT


def schedule():
    at, slot, mod, ring, ffn, tile = {}, 0, 0, 0, 0, 0
    for l in range(DEPTH):
        for i, part in enumerate(("ffn0", "mix", "ffn1")):
            n = 3 * l + i
            if n:
                at["norm", n] = dict(mod=mod)
                mod += 1
            if part == "mix":
                at[l, "in"] = dict(slot=slot)
                slot += IN_SLOTS
                at[l, "out"] = dict(slot=slot, tile=tile)
                slot += OUT_SLOTS
            else:
                f = int(part[3])
                mods = RING_MODS[l, f]
                at[l, "up", f] = dict(slot=slot, mod=mod, ring=ring, ffn=ffn, mods=mods)
                slot += UP_SLOTS
                mod += mods
                ring += mods
                at[l, "down", f] = dict(slot=slot, ffn=ffn, tile=tile)
                slot += DOWN_SLOTS
                ffn += 1
            tile += KD
    assert slot == SLOTS and mod == len(ADA_ORDER)
    return at


AT = schedule()


def build(nc, x_t, params, head_w, ada_w, weights, gate_w, sgu_w, sgu_b, out):
    with ExitStack() as ctx:
        def sb(name, shape, dt=F32, scope=ctx):
            return scope.enter_context(nc.sbuf_tensor(name, shape, dt))

        def sem(name):
            return ctx.enter_context(nc.semaphore(name))

        res = sb("res", [P, KD, T])
        with ExitStack() as ada_scope:
            ada_z = sb("ada_z", [P, KD, SLOT], F32, ada_scope)
        z_hi = sb("z_hi", [P, KD, T], F32R)
        z_lo = sb("z_lo", [P, KD, T], F32R)
        raw = sb("raw", [P, RING, SLOT])
        w_hi = sb("w_hi", [P, RING, SLOT], F32R)
        w_lo = sb("w_lo", [P, RING, SLOT], F32R)
        ada_raw = sb("ada_raw", [P, ADA_RING, HALF])
        ada_acc = sb("ada_acc", [P, 2, HALF])
        sel = sb("sel", [P, 2, 32])
        ada_turned = sb("ada_turned", [P, KD, 32])
        scr = sb("scr", [P, 3, T])
        mods = sb("mods", [P, DEPTH * NMOD * KD, 2])
        n_gain = sb("n_gain", [P, DEPTH * 3, KD, 2])
        n_shift = sb("n_shift", [P, DEPTH * 3, KD, 2])
        gates = sb("gates", [P, DEPTH * 3, KD, 2])
        par = sb("par", [P, N_PAR])
        c_cols = sb("c_cols", [P, KD, 32])
        ident = sb("ident", [P, P])
        ones = sb("ones", [P, P])
        lam_t = sb("lam_t", [P, 6, DEPTH * 2 * LT])
        half_b = sb("half_b", [P, 2, DEPTH * 2 * LT])
        tok = sb("tok", [P, 4])
        tokr = sb("tokr", [P, 4])
        mhalf = sb("mhalf", [P, 4])
        bn6 = sb("bn6", [P, 4, 6])
        bn2 = sb("bn2", [P, 4, 2])

        with ExitStack() as head_scope:
            ada_head = sb("ada_head", [P, KD, KD * 2 * P], F32, head_scope)
            head_sq = sb("head_sq", [P, KD, T], F32, head_scope)
        with ExitStack() as ffn_scope:
            h_hi = sb("h_hi", [P, KF, T], F32R, ffn_scope)
            h_lo = sb("h_lo", [P, KF, T], F32R, ffn_scope)
        with ExitStack() as y_scope:
            y_hi = sb("y_hi", [P, KD, T], F32R, y_scope)
            y_lo = sb("y_lo", [P, KD, T], F32R, y_scope)
        l_s = sb("l_s", [P, 4, T])
        l_q = sb("l_q", [P, 4, T])
        l_bx = sb("l_bx", [P, 4, T])
        l_a = sb("l_a", [P, 4, T])
        y_lru = sb("y_lru", [P, LT, T])
        gl = sb("gl", [P, LT, T])
        v_n = sb("v_n", [P, 4, 512])
        y_sgu = sb("y_sgu", [P, LT, T])
        xpad = sb("xpad", [P, 2, 2, SEQ + 3])
        xc = sb("xc", [P, LT, T])
        bd = sb("bd", [P, 16, P])
        ws = sb("ws", [P, LT, P])
        bs = sb("bs", [P, LT, P])

        bank = [ctx.enter_context(nc.psum_tensor(f"bank{i}", [P, 512], F32)) for i in range(8)]
        pa, po, p_ada, p_misc = bank[0:4], bank[4:6], bank[6], bank[7]
        x_bank = pa[0:2] + po

        raw_in = [sem(f"raw_in{i}") for i in range(RING)]
        ada_in = [sem(f"ada_in{i}") for i in range(ADA_RING)]
        hi_ready, lo_ready, slot_done = sem("hi_ready"), sem("lo_ready"), sem("slot_done")
        pre_in = [sem(f"pre_in{i}") for i in range(4)]
        acc_done, acc_read, pre_done = sem("acc_done"), sem("acc_read"), sem("pre_done")
        turned, mods_ready = sem("turned"), sem("mods_ready")
        head_in = [sem(f"head_in{i}") for i in range(KD)]
        head_sum, head_mm, head_turned = sem("head_sum"), sem("head_mm"), sem("head_turned")
        par_in, x_in, out_done, mix_in = sem("par_in"), sem("x_in"), sem("out_done"), sem("mix_in")
        const_ready, cvec_ready = sem("const_ready"), sem("cvec_ready")
        prepped, pool_chain, dve_chain, act_chain = sem("prepped"), sem("pool_chain"), sem("dve_chain"), sem("act_chain")
        silu_ready, hid_ready = sem("silu_ready"), sem("hid_ready")
        hid_hi_ready, hid_lo_ready = sem("hid_hi_ready"), sem("hid_lo_ready")
        res_ready, sq_ready, sqsum_ready = sem("res_ready"), sem("sq_ready"), sem("sqsum_ready")
        ss_done, var_ready, rstd_ready = sem("ss_done"), sem("var_ready"), sem("rstd_ready")
        diag_ready, bcast_done = sem("diag_ready"), sem("bcast_done")
        zt_ready, z_hi_ready, z_full_ready = sem("zt_ready"), sem("z_hi_ready"), sem("z_full_ready")
        z_ready = [sem("z_even_ready"), sem("z_odd_ready")]
        copy_ready, xc_ready, gate_mm = sem("copy_ready"), sem("xc_ready"), sem("gate_mm")
        ti_ready, exp_ready, bx_ready = sem("ti_ready"), sem("exp_ready"), sem("bx_ready")
        sqrt_ready, scan_ready = sem("sqrt_ready"), sem("scan_ready")
        gelu_ready, vvar_ready, vrstd_ready = sem("gelu_ready"), sem("vvar_ready"), sem("vrstd_ready")
        vn_ready, spatial_mm, zz_ready = sem("vn_ready"), sem("spatial_mm"), sem("zz_ready")
        y_ready, y_hi_ready = sem("y_ready"), sem("y_hi_ready")
        y_lo_dve, y_lo_pool = sem("y_lo_dve"), sem("y_lo_pool")
        lam_ready, bd_zero = sem("lam_ready"), sem("bd_zero")
        block = ctx.enter_context(nc.Block())

        HID0 = 2
        ACC0 = 1
        MODS0 = 1
        HID_LO0 = 1

        def dft(n):
            return SEQ if n >= 5 else T

        def streams(width):
            return 1 if width == SEQ else 2

        @block.sync
        def _(sp):
            def slot_dma(s, r):
                if isinstance(s, int) and s >= SLOTS:
                    return
                if not isinstance(s, int) or s >= RING:
                    sp.wait_ge(lo_ready, s - (RING - 1))
                src = weights[s] if isinstance(s, int) else weights[bass.ds(s, 1)].rearrange("a p n -> p (a n)")
                sp.dma_start(raw[:, r, :], src).then_inc(raw_in[r], 16)

            def piece(mod, p, r):
                u = mod * KD + 2 * (p % 4) + r
                c = slice((p // 4) * HALF, (p // 4 + 1) * HALF)
                src = ada_w[u, :, c] if isinstance(u, int) else ada_w[bass.ds(u, 1), :, c].rearrange("a p n -> p (a n)")
                sp.dma_start(ada_raw[:, r, :], src).then_inc(ada_in[r], 16)

            def piece_dma(at, i, p):
                if p < KD - 1:
                    mod = at["mod"] + i
                elif isinstance(i, int) and i == at["mods"] - 1:
                    nxt = [a for a in ring_stages if a["ring"] > at["ring"]]
                    if not nxt:
                        return
                    mod = nxt[0]["mod"]
                else:
                    mod = at["mod"] + i + 1
                for r in range(2):
                    sp.wait_ge(acc_done, ((at["ring"] + i) * KD + p) * 4 + 2 * r + 2)
                    piece(mod, (p + 1) % KD, r)

            def pre_dma(n, pairs):
                for i in pairs:
                    u = AT["norm", n]["mod"] * KD + 2 * i
                    sp.dma_start(ada_z[:, 2 * i:2 * i + 2, :],
                                 ada_w[u:u + 2].rearrange("a p n -> p a n")).then_inc(pre_in[i], 16)

            def stage(base):
                def body(i):
                    for q in range(4):
                        slot_dma(base + 8 + i * 4 + q, q)
                return body

            def ring_mod(at):
                def body(i):
                    for p in range(KD):
                        piece_dma(at, i, p)
                        slot_dma(at["slot"] + 12 + i * KD + p, p % RING)
                return body

            def run(body, n, peel):
                if n - peel > 0:
                    with sp.Fori(0, n - peel) as i:
                        body(i)
                for i in range(n - peel, n):
                    body(i)

            ring_stages = [AT[l, "up", f] for l in range(DEPTH) for f in range(2) if AT[l, "up", f]["mods"]]
            sp.dma_start(par[:], params).then_inc(par_in, 16)
            sp.dma_start(res[:], x_t).then_inc(x_in, 16)
            for k in range(KD):
                sp.dma_start(ada_head[:, k, :], head_w[k]).then_inc(head_in[k], 16)
                if k == 0:
                    for s in range(RING):
                        slot_dma(s, s)
            for s in range(RING, 8):
                slot_dma(s, s % RING)
            for r in range(ADA_RING):
                piece(0, 0, r)
            for l in range(DEPTH):
                for f in range(2):
                    up, down = AT[l, "up", f], AT[l, "down", f]
                    stage(up["slot"])(0)
                    if up["mods"]:
                        run(ring_mod(up), up["mods"], 1)
                    run(stage(up["slot"] + 4 + KD * up["mods"]), UP_SLOTS // 4 - 1 - 2 * up["mods"], 0)
                    final = l == DEPTH - 1 and f == 1
                    if final:
                        run(stage(down["slot"]), DOWN_SLOTS // 4, 2)
                        continue
                    body = stage(down["slot"])
                    for i in range(4):
                        body(i)
                        if i == 0:
                            sp.wait_ge(slot_done, down["slot"])
                        pre_dma(3 * l + 2 * f + 1, (i,))
                    with sp.Fori(4, DOWN_SLOTS // 4) as i:
                        body(i)
                    if f == 0:
                        sp.wait_ge(slot_done, down["slot"] + DOWN_SLOTS)
                        sp.wait_ge(bd_zero, l + 1)
                        for a in range(2):
                            sp.dma_start(bd[64 * a:64 * a + 64, :, 64 * a:64 * a + 64], gate_w[l, a]).then_inc(mix_in, 16)
                        sp.dma_start(ws[:], sgu_w[l]).then_inc(mix_in, 16)
                        sp.dma_start(bs[:], sgu_b[l].partition_broadcast(P)).then_inc(mix_in, 16)
                        body = stage(AT[l, "in"]["slot"])
                        run(body, IN_SLOTS // 4, 0)
                        sp.wait_ge(slot_done, AT[l, "out"]["slot"])
                        for i in range(2):
                            pre_dma(3 * l + 2, (2 * i, 2 * i + 1))
                            body(IN_SLOTS // 4 + i)
            for k in range(0, KD, 2):
                sp.wait_ge(zt_ready, 6 * KD + k + 2)
                sp.dma_start(out[:, k:k + 2, :], res[:, k:k + 2, 0:SEQ]).then_inc(out_done, 16)
            sp.wait_ge(out_done, 16 * KD // 2)

        @block.tensor
        def _(pe):
            def product(bank_ap, blk, r, rhs_hi, rhs_lo, start, stop):
                c = slice(blk * P, (blk + 1) * P)
                pe.matmul(bank_ap, w_hi[:, r, c], rhs_hi, start=start, stop=False)
                pe.matmul(bank_ap, w_hi[:, r, c], rhs_lo, start=False, stop=False)
                return pe.matmul(bank_ap, w_lo[:, r, c], rhs_hi, start=False, stop=stop)

            def ada_unit(dst, data, k):
                w = data.rearrange("p (b j i) -> p b j i", b=KD, j=4)
                for j in range(4):
                    m = pe.matmul(dst[32 * j:32 * j + 32, 0:256], c_cols[:, k, :], w[:, :, j, :],
                                  start=(k == 0), stop=(k == KD - 1), tile_position=(0, 32 * j))
                return m

            def ring_sum(at, i, h):
                if h == 0:
                    pe.wait_ge(mods_ready, MODS0 + at["mod"] + i)
                pe.wait_ge(acc_done, ((at["ring"] + i) * 2 + h + 1) * 16)
                w = ada_acc.rearrange("p s (b j i) -> p s b j i", b=4, j=4)
                for s in range(2):
                    for j in range(4):
                        m = pe.matmul(p_ada[32 * j:32 * j + 32, h * P:(h + 1) * P], sel[:, s, :], w[:, s, :, j, :],
                                      start=(s == 0), stop=(s == 1), tile_position=(0, 32 * j))
                m.then_inc(acc_read, 1)

            def gap_unit(n, k):
                if n == 3 * DEPTH:
                    return
                if k == 0:
                    pe.wait_ge(mods_ready, MODS0 + AT["norm", n]["mod"])
                if k % 2 == 0:
                    pe.wait_ge(pre_in[k // 2], 16 * n)
                m = ada_unit(p_ada, ada_z[:, k, :], k)
                if k == KD - 1:
                    m.then_inc(pre_done, 1)

            def norm(n):
                w = dft(n)
                if n == 0:
                    pe.wait_ge(const_ready, 1)
                if n == 0:
                    pe.wait_ge(head_sum, KD - 1)
                    for m in range(w // P):
                        mm = pe.matmul(po[0][:, m:m + 1], scr[:, 2, m * P:(m + 1) * P], ones[:, 0:1],
                                       start=(m == 0), stop=True, skip_group_check=True)
                else:
                    for k in range(0, 2):
                        gap_unit(n, k)
                    pe.wait_ge(sqsum_ready, 6 * n)
                    pe.wait_ge(res_ready, HID0 + KD * n)
                    for src in (2, 1):
                        if src == 1:
                            pe.wait_ge(sq_ready, KD * (n + 1))
                        for m in range(w // P):
                            mm = pe.matmul(po[0][:, m:m + 1], scr[:, src, m * P:(m + 1) * P], ones[:, 0:1],
                                           start=(src == 2 and m == 0), stop=(src == 1), skip_group_check=True)
                mm.then_inc(ss_done, 1)
                for k in range(2, 5 if n else 2):
                    gap_unit(n, k)
                pe.wait_ge(diag_ready, n + 1)
                pe.matmul(po[1][:, 0:w], ones[:], scr[:, 0, 0:w], start=True, stop=True).then_inc(bcast_done, 1)
                for k in range(5, KD if n else 5):
                    gap_unit(n, k)

            def head_unit(b):
                if b >= 2:
                    pe.wait_ge(head_turned, b - 1)
                pe.wait_ge(head_in[b], 16)
                w = ada_head[:, b, :].rearrange("p (k m j i) -> p k m j i", k=KD, m=2, j=4)
                for k in range(KD):
                    for j in range(4):
                        m = pe.matmul((p_ada, p_misc)[b % 2][32 * j:32 * j + 32, 0:64], c_cols[:, k, :], w[:, k, :, j, :],
                                      start=(k == 0), stop=(k == KD - 1), tile_position=(0, 32 * j))
                m.then_inc(head_mm, 1)

            def first_slots(n, base, banks):
                w = dft(n)
                for q in range(len(banks)):
                    pe.wait_ge(lo_ready, base + q + 1)
                for k in range(KD):
                    if n == 0 and k + 2 < KD:
                        head_unit(k + 2)
                    pe.wait_ge(z_ready[k % 2], KD // 2 * n + k // 2 + 1)
                    for q, dst in enumerate(banks):
                        m = product(dst[:, 0:w], k, q, z_hi[:, k, 0:w], z_lo[:, k, 0:w], k == 0, k == KD - 1)
                        if k == KD - 1:
                            m.then_inc(slot_done, 1)

            def up_stage(l, f):
                at = AT[l, "up", f]
                n = 3 * l + 2 * f
                w = dft(n)

                def slot(i, p):
                    q = p % 4
                    j2 = at["ffn"] * KF + i * 2 + p // 2
                    pe.wait_ge(lo_ready, at["slot"] + i * 4 + p + 1)
                    if q % 2 == 0:
                        pe.wait_ge(hid_ready, HID0 - 1 + j2)
                    for k in range(KD):
                        m = product(pa[q][:, 0:w], k, q, z_hi[:, k, 0:w], z_lo[:, k, 0:w], k == 0, k == KD - 1)
                    m.then_inc(slot_done, 1)

                side = HEAD_SIDE if n == 0 else SIDE
                pe.wait_ge(hid_ready, HID0 + at["ffn"] * KF)
                first_slots(n, at["slot"], pa[0:side])
                for p in range(side, 4):
                    slot(0, p)
                if at["mods"]:
                    with pe.Fori(0, at["mods"]) as i:
                        for p in range(KD):
                            slot(i * 2 + 1, p)
                            if p % 4 == 3:
                                ring_sum(at, i, p // 4)
                if 1 + 2 * at["mods"] < UP_SLOTS // 4:
                    with pe.Fori(1 + 2 * at["mods"], UP_SLOTS // 4) as i:
                        for p in range(4):
                            slot(i, p)

            def down_stage(l, f):
                at = AT[l, "down", f]
                w = dft(3 * l + 2 * f)
                with pe.Fori(0, 2) as i:
                    for dd in range(4):
                        for part, n_blk in enumerate((8, 8, 6)):
                            q = 3 * dd + part
                            pe.wait_ge(lo_ready, at["slot"] + 1 + i * 12 + q)
                            if part == 0:
                                pe.wait_ge(res_ready, HID0 - 1 + at["tile"] + i * 4 + dd)
                            for b in range(n_blk):
                                k = 8 * part + b
                                if dd == 0 and k in (0, KF - 2, KF - 1):
                                    pe.wait_ge(hid_lo_ready, HID_LO0 + at["ffn"] * KF + max(k + 1, KF - 2))
                                m = product(po[dd % 2][:, 0:w], b, q % RING, h_hi[:, k, 0:w], h_lo[:, k, 0:w],
                                            k == 0, k == KF - 1)
                            m.then_inc(slot_done, 1)

            def in_stage(l):
                at = AT[l, "in"]
                n = 3 * l + 1
                wl = SEQ if l == DEPTH - 1 else T
                pe.wait_ge(hid_ready, HID0 + KF * (2 * l + 1))
                first_slots(n, at["slot"], x_bank[0:SIDE])
                for q in range(SIDE, IN_SLOTS):
                    pe.wait_ge(lo_ready, at["slot"] + q + 1)
                    kind, t = q // 4, q % 4
                    if q == 3:
                        pe.wait_ge(zt_ready, KD * (n + 1))
                    if q == 4:
                        pe.wait_ge(copy_ready, 8 * l + 2)
                    if kind == 2:
                        pe.wait_ge(copy_ready, 8 * l + t + 3)
                    if q == 12:
                        pe.wait_ge(vn_ready, l + 1)
                    w = T if kind == 0 else wl
                    if kind == 1:
                        for kk in range(2):
                            k = 2 * t + kk
                            c = slice(kk * 512, kk * 512 + 512)
                            for m_ in range(wl // P):
                                tk = slice(m_ * P, m_ * P + P)
                                pe.matmul(pa[m_][:], z_hi[:, k, tk], w_hi[:, q % 4, c], start=(k == 0), stop=False)
                                pe.matmul(pa[m_][:], z_lo[:, k, tk], w_hi[:, q % 4, c], start=False, stop=False)
                                m = pe.matmul(pa[m_][:], z_hi[:, k, tk], w_lo[:, q % 4, c], start=False, stop=(k == KD - 1))
                    else:
                        dst = {0: x_bank, 2: (po * 2), 3: pa}[kind][t]
                        for k in range(KD):
                            m = product(dst[:, 0:w], k, q % 4, z_hi[:, k, 0:w], z_lo[:, k, 0:w], k == 0, k == KD - 1)
                    m.then_inc(slot_done, 1)
                    if 4 <= q < 12:
                        u = q - 4
                        t_, d_ = u // 2, u % 2
                        pe.wait_ge(xc_ready, 4 * l + t_ + 1)
                        if u == 0:
                            pe.wait_ge(mix_in, 64 * (l + 1))
                            pe.wait_ge(mods_ready, MODS0 + AT["norm", n]["mod"] + 1)
                        if u or l:
                            pe.wait_ge(ti_ready, 8 * l + u)
                        for kind_, dst in ((0, p_ada), (1, p_misc)):
                            m = pe.matmul(dst[:], bd[:, kind_ * 8 + d_ * 4 + t_, :], xc[:, t_, :], start=True, stop=True)
                        m.then_inc(gate_mm, 1)
                    if q >= 12:
                        g = q - 12
                        if g < 2:
                            pe.wait_ge(ti_ready, 8 * (l + 1))
                        else:
                            pe.wait_ge(zz_ready, 4 * l + g - 1)
                        dst = (p_ada, p_misc)[g % 2]
                        for m_ in range(wl // P):
                            m = pe.matmul(dst[:, m_ * P:(m_ + 1) * P], v_n[:, m_, g * P:(g + 1) * P], ws[:, g, :],
                                          start=True, stop=True)
                        m.then_inc(spatial_mm, 1)

            def out_stage(l):
                at = AT[l, "out"]
                w = SEQ if l == DEPTH - 1 else T
                def slot(i, q):
                    pe.wait_ge(lo_ready, at["slot"] + 1 + i * 4 + q)
                    pe.wait_ge(res_ready, HID0 - 1 + at["tile"] + i * 4 + q)
                    for k in range(KD):
                        m = product(po[q % 2][:, 0:w], k, q, y_hi[:, k, 0:w], y_lo[:, k, 0:w], k == 0, k == KD - 1)
                    m.then_inc(slot_done, 1)

                pe.wait_ge(copy_ready, 8 * (l + 1))
                pe.wait_ge(lo_ready, at["slot"] + 2)
                pe.wait_ge(res_ready, HID0 + at["tile"])
                for n_, k in enumerate(Y_ORDER):
                    if n_ < Y_POOL:
                        pe.wait_ge(y_lo_pool, Y_POOL * l + n_ + 1)
                    else:
                        pe.wait_ge(y_lo_dve, (KD - Y_POOL) * l + n_ - Y_POOL + 1)
                    for q in range(2):
                        m = product(po[q][:, 0:w], k, q, y_hi[:, k, 0:w], y_lo[:, k, 0:w], n_ == 0, n_ == KD - 1)
                        if n_ == KD - 1:
                            m.then_inc(slot_done, 1)
                for q in range(2, 4):
                    slot(0, q)
                for q in range(4):
                    slot(1, q)

            pe.wait_ge(cvec_ready, 1)
            head_unit(0)
            norm(0)
            head_unit(1)
            for l in range(DEPTH):
                up_stage(l, 0)
                down_stage(l, 0)
                norm(3 * l + 1)
                in_stage(l)
                out_stage(l)
                norm(3 * l + 2)
                up_stage(l, 1)
                down_stage(l, 1)
                norm(3 * l + 3)

        @block.scalar
        def _(act):
            def split_hi(s, r):
                if isinstance(s, int) and s >= SLOTS:
                    return
                if isinstance(s, int):
                    act.wait_ge(raw_in[r], 16 * (s // RING + 1))
                act.activation(w_hi[:, r, :], raw[:, r, :], ACT.Copy).then_inc(hi_ready, 1)

            def hi_in_loop(base, i, per, q):
                r = q % RING
                act.wait_ge(raw_in[r], 16 * ((base + q) // RING + 2) + i * (16 * per // RING))
                act.activation(w_hi[:, r, :], raw[:, r, :], ACT.Copy).then_inc(hi_ready, 1)

            def square(d, n):
                w = dft(n)
                if n:
                    act.wait_ge(res_ready, HID0 + KD * (n - 1) + d + 1)
                if n and d >= 3:
                    act.wait_ge(sqsum_ready, 6 * (n - 1) + d - 2)
                dst = head_sq[:, d, :] if n == 0 else scr[:, 2 if d == 0 else d % 2, 0:w]
                act.activation(dst, res[:, d, 0:w], ACT.Square).then_inc(sq_ready, 1)

            def norm(n):
                if n == 3 * DEPTH:
                    return
                w = dft(n)
                for k in range(KD):
                    act.wait_ge(zt_ready, KD * n + k + 1)
                    for s in range(streams(w)):
                        c = slice(s * SEQ, (s + 1) * SEQ)
                        m = act.activation(z_hi[:, k, c], scr[:, k % 3, c], ACT.Identity, bias=n_shift[:, n, k, s:s + 1])
                    m.then_inc(z_hi_ready, 1)
                    if k % 2 and n:
                        act.wait_ge(z_hi_ready, KD * n + k + 1)
                        for s in range(streams(w)):
                            c = slice(s * SEQ, (s + 1) * SEQ)
                            m = act.activation(scr[:, k % 3, c], scr[:, k % 3, c], ACT.Identity,
                                               bias=n_shift[:, n, k, s:s + 1])
                        m.then_inc(z_full_ready, 1)

            def up_stage(l, f):
                at = AT[l, "up", f]
                w = dft(3 * l + 2 * f)
                with act.Fori(0, UP_SLOTS // 4) as i:
                    for q in range(4):
                        j = at["ffn"] * KF + i * 2 + q // 2
                        act.wait_ge(slot_done, at["slot"] + 1 + i * 4 + q)
                        if q % 2 == 0:
                            hi_in_loop(at["slot"], i, 4, q)
                            act.activation(scr[:, q // 2, 0:w], pa[q][:, 0:w], ACT.Silu).then_inc(silu_ready, 1)
                        else:
                            hi_in_loop(at["slot"], i, 4, q)
                            act.wait_ge(hid_ready, HID0 + 1 + j)
                            act.activation(h_hi[:, bass.ds(i * 2 + q // 2, 1), 0:w].rearrange("p a n -> p (a n)"),
                                           scr[:, 2, 0:w], ACT.Copy).then_inc(hid_hi_ready, 1)

            def down_stage(l, f):
                at = AT[l, "down", f]
                for q in range(DOWN_SLOTS):
                    act.wait_ge(slot_done, at["slot"] + q + 1)
                    split_hi(at["slot"] + q + 4, q % 4)
                    if q % 3 == 2:
                        square(q // 3, 3 * l + 2 * f + 1)

            def in_stage(l):
                at = AT[l, "in"]
                wl = SEQ if l == DEPTH - 1 else T
                ns = wl // SEQ
                for q in range(IN_SLOTS):
                    act.wait_ge(slot_done, at["slot"] + q + 1)
                    kind, t = q // 4, q % 4
                    if kind == 0:
                        if t >= 2:
                            act.wait_ge(xc_ready, 4 * l + t - 1)
                        elif t == 0:
                            act.wait_ge(bd_zero, l + 1)
                        act.activation(xpad[:, t % 2, :, 2:2 + SEQ], x_bank[t].rearrange("p (s n) -> p s n", s=2),
                                       ACT.Copy).then_inc(copy_ready, 1)
                    if kind == 2:
                        act.activation(gl[:, t, 0:wl], po[t % 2][:, 0:wl], ACT.Copy).then_inc(copy_ready, 1)
                    if q not in MIX_HI_DVE:
                        s = at["slot"] + q + 4
                        if q > 0:
                            act.wait_ge(hi_ready, s)
                        split_hi(s, q % 4)
                    if 4 <= q < 12:
                        u = q - 4
                        t_, d_ = u // 2, u % 2
                        c = l * 8 + d_ * 4 + t_
                        r = u % 4
                        act.wait_ge(gate_mm, 8 * l + u + 1)
                        if u >= 4:
                            act.wait_ge(scan_ready, 4 * l + t_ - 1)
                        elif u == 0:
                            act.wait_ge(lam_ready, 3)
                        act.activation(l_q[:, r, :], p_ada[:], ACT.Tanh, bias=half_b[:, 0, c:c + 1], scale=0.5).then_inc(act_chain, 1)
                        act.activation(l_bx[:, r, :], p_misc[:], ACT.Tanh, bias=half_b[:, 1, c:c + 1], scale=0.5).then_inc(ti_ready, 1)
                        act.wait_ge(act_chain, 2 * (8 * l + u) + 1)
                        act.activation(l_s[:, r, :], l_q[:, r, :], ACT.Tanh, bias=lam_t[:, 4, c:c + 1],
                                       scale=lam_t[:, 4, c:c + 1]).then_inc(act_chain, 1)
                        act.activation(l_a[:, r, :], l_q[:, r, :], ACT.Exp, bias=lam_t[:, 5, c:c + 1],
                                       scale=lam_t[:, 5, c:c + 1]).then_inc(exp_ready, 1)
                        if d_ == 1:
                            for u_ in (u - 1, u):
                                act.wait_ge(act_chain, 2 * (8 * l + u_) + 2)
                                act.activation(l_s[:, u_ % 4, :], l_s[:, u_ % 4, :], ACT.Sqrt).then_inc(sqrt_ready, 1)
                    if q == 12:
                        for t_ in range(LT):
                            act.wait_ge(copy_ready, 8 * (l + 1))
                            act.activation(gl[:, t_, 0:wl], gl[:, t_, 0:wl], ACT.Gelu_apprx_tanh).then_inc(gelu_ready, 1)
                for n_, k in enumerate(Y_ORDER):
                    act.wait_ge(y_ready, 8 * l + n_ + 1)
                    src = y_lru if k < 4 else y_sgu
                    act.activation(y_hi[:, k, 0:wl], src[:, k % 4, 0:wl], ACT.Copy).then_inc(y_hi_ready, 1)

            def out_stage(l):
                at = AT[l, "out"]
                for q in range(OUT_SLOTS):
                    act.wait_ge(slot_done, at["slot"] + q + 1)
                    split_hi(at["slot"] + q + 4, q % 4)
                    square(q, 3 * l + 2)

            act.wait_ge(par_in, 16)
            act.wait_ge(const_ready, 1)
            act.wait_ge(lam_ready, 1)
            act.activation(lam_t[:, 1, :], lam_t[:, 0, :], ACT.Exp, scale=-1.0).then_inc(lam_ready, 1)
            act.activation(c_cols[:, :, 0:2], par[:, C_CVEC:C_CVEC + 2 * KD].rearrange("p (k s) -> p k s", s=2),
                           ACT.Silu).then_inc(cvec_ready, 1)
            act.wait_ge(x_in, 16)
            for d in range(KD):
                square(d, 0)
            for s in range(RING):
                split_hi(s, s)
            norm(0)
            for l in range(DEPTH):
                up_stage(l, 0)
                down_stage(l, 0)
                norm(3 * l + 1)
                in_stage(l)
                out_stage(l)
                norm(3 * l + 2)
                up_stage(l, 1)
                down_stage(l, 1)
                norm(3 * l + 3)

        @block.vector
        def _(dve):
            chain = [0]

            def link(ins):
                chain[0] += 1
                ins.then_inc(dve_chain, 1)
                dve.wait_ge(dve_chain, chain[0])

            def split_lo(s, r):
                if isinstance(s, int) and s >= SLOTS:
                    return
                dve.wait_ge(hi_ready, s + 1)
                dve.tensor_tensor(w_lo[:, r, :], raw[:, r, :], w_hi[:, r, :].bitcast(F32), ALU.subtract).then_inc(lo_ready, 1)

            def ada_turn(mod):
                dve.wait_ge(mods_ready, MODS0 + mod)
                dve.transpose(ada_turned.rearrange("p b r -> p (b r)"), p_ada[:, 0:256]).then_inc(turned, 1)
                dve.wait_ge(turned, mod + 1)
                dst = mods[:, mod * KD:mod * KD + KD, :] if isinstance(mod, int) else mods[:, bass.ds(mod * KD, KD), :]
                dve.tensor_copy(dst, ada_turned[:, :, 0:2]).then_inc(mods_ready, 1)

            def gap_turn(n):
                dve.wait_ge(pre_done, n)
                ada_turn(AT["norm", n]["mod"])

            def residual(l, norm_i, d, w, tile):
                if d == 0:
                    dve.wait_ge(prepped, 6 * l + 2 * norm_i + 1)
                for s in range(streams(w)):
                    c = slice(s * SEQ, (s + 1) * SEQ)
                    m = dve.scalar_tensor_tensor(res[:, d, c], po[d % 2][:, c], gates[:, 3 * l + norm_i, d, s:s + 1],
                                                 res[:, d, c], ALU.mult, ALU.add)
                m.then_inc(res_ready, 1)

            def norm(n):
                w = dft(n)
                m4 = w // P
                if n == 0:
                    for d in range(1, KD):
                        dve.wait_ge(sq_ready, d + 1)
                        if d > 1:
                            dve.wait_ge(head_sum, d - 1)
                        dve.tensor_tensor(scr[:, 2, :], head_sq[:, 0, :] if d == 1 else scr[:, 2, :], head_sq[:, d, :],
                                          ALU.add).then_inc(head_sum, 1)
                    split_lo(0, 0)
                dve.wait_ge(ss_done, n + 1)
                dve.tensor_scalar(tok[:, 0:m4], po[0][:, 0:m4], 1.0 / D, EPS, ALU.mult, ALU.add).then_inc(var_ready, 1)
                if n == 0:
                    split_lo(1, 1)
                dve.wait_ge(rstd_ready, n + 1)
                dve.tensor_tensor(scr[:, 0, 0:w].rearrange("p (m j) -> p m j", j=P),
                                  ident[:].unsqueeze(1).to_broadcast([P, m4, P]),
                                  tokr[:, 0:m4].unsqueeze(2).to_broadcast([P, m4, P]), ALU.mult).then_inc(diag_ready, 1)
                if n == 0:
                    split_lo(2, 2)
                    split_lo(3, 3)
                dve.wait_ge(bcast_done, n + 1)
                if 0 < n < 3 * DEPTH:
                    dve.wait_ge(prepped, 2 * n)
                if n == 3 * DEPTH:
                    for k in range(KD):
                        g = C_GAIN + n * KD + k
                        dve.scalar_tensor_tensor(res[:, k, 0:w], res[:, k, 0:w], par[:, g:g + 1], po[1][:, 0:w],
                                                 ALU.mult, ALU.mult).then_inc(zt_ready, 1)
                    return

                def scaled(k):
                    if k >= 3:
                        dve.wait_ge(z_ready[(k - 3) % 2], KD // 2 * n + (k - 3) // 2 + 1)
                    for s in range(streams(w)):
                        c = slice(s * SEQ, (s + 1) * SEQ)
                        m = dve.scalar_tensor_tensor(scr[:, k % 3, c], res[:, k, c], n_gain[:, n, k, s:s + 1],
                                                     po[1][:, c], ALU.mult, ALU.mult)
                    m.then_inc(zt_ready, 1)

                def z_low(k):
                    dve.wait_ge(z_hi_ready, KD * n + k + 1)
                    for s in range(streams(w)):
                        c = slice(s * SEQ, (s + 1) * SEQ)
                        m = dve.scalar_tensor_tensor(z_lo[:, k, c], scr[:, k % 3, c], n_shift[:, n, k, s:s + 1],
                                                     z_hi[:, k, c].bitcast(F32), ALU.add, ALU.subtract)
                    m.then_inc(z_ready[k % 2], 1)

                def head_turn(b):
                    dve.wait_ge(head_mm, b + 1)
                    dve.transpose(ada_turned[:, 0:2, :].rearrange("p b r -> p (b r)"),
                                  (p_ada, p_misc)[b % 2][:, 0:64]).then_inc(head_turned, 1)
                    dve.wait_ge(head_turned, b + 1)

                    def bias(m):
                        c = C_BADA + m * KD + b
                        return par[:, c:c + 1].to_broadcast([P, 2])
                    dve.tensor_tensor(n_shift[:, 0, b, :], ada_turned[:, 0, 0:2], bias(0), ALU.add)
                    link(dve.scalar_tensor_tensor(n_gain[:, 0, b, :], ada_turned[:, 1, 0:2], 1.0, bias(1), ALU.add, ALU.add))
                    m = dve.tensor_scalar(n_gain[:, 0, b, :], n_gain[:, 0, b, :], par[:, C_GAIN + b:C_GAIN + b + 1], None,
                                          ALU.mult)
                    if b == KD - 1:
                        m.then_inc(mods_ready, MODS0)
                        dve.wait_ge(mods_ready, MODS0)
                    else:
                        link(m)

                if n == 0:
                    for k in range(KD):
                        head_turn(k)
                        scaled(k)
                        z_low(k)
                    return
                scaled(0)
                for k in range(0, KD, 2):
                    scaled(k + 1)
                    if k == 0:
                        dve.wait_ge(pre_done, n)
                    z_low(k)
                    if k + 2 < KD:
                        scaled(k + 2)
                gap_turn(n)

            def up_stage(l, f):
                at = AT[l, "up", f]
                w = dft(3 * l + 2 * f)

                def slot(i, p):
                    q = p % 4
                    s = at["slot"] + i * 4 + p
                    dve.wait_ge(slot_done, s + 1)
                    if q % 2 == 1:
                        jj = i * 2 + p // 2
                        j = at["ffn"] * KF + jj
                        dve.wait_ge(silu_ready, j + 1)
                        dve.wait_ge(hid_lo_ready, HID_LO0 + j)
                        dve.tensor_tensor(scr[:, 2, 0:w], scr[:, q // 2, 0:w], pa[q][:, 0:w], ALU.mult).then_inc(hid_ready, 1)
                    split_lo(s + 4, q)
                    if q % 2 == 1:
                        dve.wait_ge(hid_hi_ready, j + 1)
                        hid = slice(jj, jj + 1) if isinstance(jj, int) else bass.ds(jj, 1)
                        dve.tensor_tensor(h_lo[:, hid, 0:w].rearrange("p a n -> p (a n)"), scr[:, 2, 0:w],
                                          h_hi[:, hid, 0:w].rearrange("p a n -> p (a n)").bitcast(F32),
                                          ALU.subtract).then_inc(hid_lo_ready, 1)

                def ring_pieces(i, p):
                    ring = at["ring"] + i
                    for r in range(2):
                        k = 2 * (p % 4) + r
                        dve.wait_ge(ada_in[r], (ring * KD + p + 1) * 16)
                        if k == 0:
                            dve.wait_ge(acc_read, ACC0 + ring * 2 + p // 4)
                        for st in range(2):
                            c = c_cols[:, k, st:st + 1]
                            if k == 0:
                                m = dve.tensor_scalar(ada_acc[:, st, :], ada_raw[:, r, :], c, None, ALU.mult)
                            else:
                                dve.wait_ge(acc_done, (ring * KD + p) * 4 + 2 * r + st - 1)
                                m = dve.scalar_tensor_tensor(ada_acc[:, st, :], ada_raw[:, r, :], c, ada_acc[:, st, :],
                                                             ALU.mult, ALU.add)
                            m.then_inc(acc_done, 1)

                for p in range(4):
                    slot(0, p)
                if at["mods"]:
                    with dve.Fori(0, at["mods"]) as i:
                        for p in range(KD):
                            ring_pieces(i, p)
                            slot(i * 2 + 1, p)
                        dve.wait_ge(acc_read, ACC0 + (at["ring"] + i + 1) * 2)
                        ada_turn(at["mod"] + i)
                if 1 + 2 * at["mods"] < UP_SLOTS // 4:
                    with dve.Fori(1 + 2 * at["mods"], UP_SLOTS // 4) as i:
                        for p in range(4):
                            slot(i, p)

            def down_stage(l, f):
                at = AT[l, "down", f]
                w = dft(3 * l + 2 * f)
                for q in range(DOWN_SLOTS):
                    dve.wait_ge(slot_done, at["slot"] + q + 1)
                    if q % 3 == 2:
                        residual(l, 2 * f, q // 3, w, at["tile"])
                    split_lo(at["slot"] + q + 4, q % 4)

            def conv(l, t):
                dve.wait_ge(copy_ready, 8 * l + t + 1)
                o = xc[:, t, :].rearrange("p (s n) -> p s n", s=2)
                c = C_CONV + l * 5 * LT + t
                link(dve.tensor_scalar(o, xpad[:, t % 2, :, 0:SEQ], par[:, c:c + 1], par[:, c + 4 * LT:c + 4 * LT + 1],
                                       ALU.mult, ALU.add))
                for k in range(1, 4):
                    m = dve.scalar_tensor_tensor(o, xpad[:, t % 2, :, k:k + SEQ], par[:, c + k * LT:c + k * LT + 1], o,
                                                 ALU.mult, ALU.add)
                    if k < 3:
                        link(m)
                m.then_inc(xc_ready, 1)

            def scans(l, t):
                for d in range(2):
                    u = 2 * t + d
                    r = u % 4
                    dve.wait_ge(exp_ready, 8 * l + u + 1)
                    dve.wait_ge(bx_ready, 8 * l + u + 1)
                    link(dve.scalar_tensor_tensor(l_q[:, r, :], l_a[:, r, :], 1.0, l_bx[:, r, :], ALU.add, ALU.mult))
                    dve.wait_ge(sqrt_ready, 8 * l + u + 1)
                    link(dve.scalar_tensor_tensor(l_q[:, r, :], l_q[:, r, :], 0.5, l_s[:, r, :], ALU.mult, ALU.mult))
                    if d == 0:
                        link(dve.tensor_tensor_scan(l_bx[:, r, SEQ:T], l_a[:, r, SEQ:T], l_q[:, r, SEQ:T], 0.0,
                                                    ALU.mult, ALU.add))
                        dve.tensor_tensor_scan(l_bx[:, r, 0:SEQ], l_a[:, r, 0:SEQ], l_q[:, r, 0:SEQ],
                                               l_bx[:, r, T - 1:T], ALU.mult, ALU.add)
                    else:
                        link(dve.tensor_tensor_scan(l_bx[:, r, ::-1], l_a[:, r, ::-1], l_q[:, r, ::-1], 0.0,
                                                    ALU.mult, ALU.add))
                r0 = (2 * t) % 4
                wl = SEQ if l == DEPTH - 1 else T
                dve.tensor_tensor(y_lru[:, t, 0:wl], l_bx[:, r0, 0:wl], l_bx[:, r0 + 1, 0:wl], ALU.add).then_inc(scan_ready, 1)

            def in_stage(l):
                at = AT[l, "in"]
                wl = SEQ if l == DEPTH - 1 else T
                m4 = wl // P
                for q in range(IN_SLOTS):
                    dve.wait_ge(slot_done, at["slot"] + q + 1)
                    s = at["slot"] + q + 4
                    if q in MIX_HI_DVE:
                        dve.wait_ge(raw_in[q % 4], 16 * (s // RING + 1))
                        dve.tensor_copy(w_hi[:, q % 4, :], raw[:, q % 4, :]).then_inc(hi_ready, 1)
                    if q < 4:
                        conv(l, q)
                    split_lo(s, q % 4)
                    if q == 7:
                        for m_ in range(m4):
                            m = dve.bn_stats(bn6[:, m_, :], pa[m_][:])
                        link(m)
                        for m_ in range(m4):
                            m = dve.bn_aggr(bn2[:, m_, :], bn6[:, m_, :])
                        m.then_inc(vvar_ready, 1)
                    if q == 9:
                        dve.wait_ge(vrstd_ready, l + 1)
                        for m_ in range(m4):
                            m = dve.tensor_scalar(v_n[:, m_, :], pa[m_][:], bn2[:, m_, 0:1], tokr[:, m_:m_ + 1],
                                                  ALU.subtract, ALU.mult)
                        m.then_inc(vn_ready, 1)
                    if q in (6, 8, 10, 12):
                        scans(l, (q - 6) // 2)
                    if q >= 12:
                        g = q - 12
                        dve.wait_ge(spatial_mm, 4 * l + g + 1)
                        src = (p_ada, p_misc)[g % 2][:, 0:wl].rearrange("p (m j) -> p m j", j=P)
                        o = y_sgu[:, g, 0:wl].rearrange("p (m j) -> p m j", j=P)
                        c = C_SGU + l * LT + g
                        if g == 0:
                            dve.wait_ge(mix_in, 64 * (l + 1))
                        dve.scalar_tensor_tensor(o, src, par[:, c:c + 1], bs[:, g, :].unsqueeze(1).to_broadcast([P, m4, P]),
                                                 ALU.mult, ALU.add).then_inc(zz_ready, 1)
                        for n_ in {0: (), 1: (0, 1, 2), 2: (3, 4, 5), 3: (6, 7)}[g]:
                            k = Y_ORDER[n_]
                            if k < 4:
                                dve.wait_ge(gelu_ready, 4 * l + k + 1)
                                dve.wait_ge(scan_ready, 4 * l + k + 1)
                                y, factor = y_lru, gl[:, k, 0:wl]
                            else:
                                dve.wait_ge(zz_ready, 4 * l + k - 3)
                                y, factor = y_sgu, pa[k - 4][:, 0:wl]
                            dve.tensor_tensor(y[:, k % 4, 0:wl], y[:, k % 4, 0:wl], factor, ALU.mult).then_inc(y_ready, 1)
                for n_ in range(Y_POOL, KD):
                    k = Y_ORDER[n_]
                    src = y_lru if k < 4 else y_sgu
                    dve.wait_ge(y_hi_ready, 8 * l + n_ + 1)
                    dve.tensor_tensor(y_lo[:, k, 0:wl], src[:, k % 4, 0:wl], y_hi[:, k, 0:wl].bitcast(F32),
                                      ALU.subtract).then_inc(y_lo_dve, 1)

            def out_stage(l):
                at = AT[l, "out"]
                w = SEQ if l == DEPTH - 1 else T
                for q in range(OUT_SLOTS):
                    dve.wait_ge(slot_done, at["slot"] + q + 1)
                    residual(l, 1, q, w, at["tile"])
                    split_lo(at["slot"] + q + 4, q % 4)

            def softplus():
                lam = par[:, C_LAM:C_LAM + DEPTH * 2 * LT]
                link(dve.tensor_scalar(lam_t[:, 0, :], lam, -1.0, None, ALU.mult))
                dve.tensor_tensor(lam_t[:, 0, :], lam_t[:, 0, :], lam, ALU.max).then_inc(lam_ready, 1)
                dve.wait_ge(lam_ready, 2)
                link(dve.tensor_scalar(lam_t[:, 2, :], lam_t[:, 1, :], 2.0, None, ALU.add))
                link(dve.reciprocal(lam_t[:, 2, :], lam_t[:, 2, :]))
                link(dve.tensor_tensor(lam_t[:, 1, :], lam_t[:, 1, :], lam_t[:, 2, :], ALU.mult))
                link(dve.tensor_tensor(lam_t[:, 2, :], lam_t[:, 1, :], lam_t[:, 1, :], ALU.mult))
                link(dve.tensor_scalar(lam_t[:, 3, :], lam_t[:, 2, :], 1.0 / 17, None, ALU.mult))
                for c in range(15, 1, -2):
                    link(dve.scalar_tensor_tensor(lam_t[:, 3, :], lam_t[:, 3, :], 1.0 / c, lam_t[:, 2, :], ALU.add, ALU.mult))
                link(dve.scalar_tensor_tensor(lam_t[:, 3, :], lam_t[:, 3, :], 1.0, lam_t[:, 1, :], ALU.add, ALU.mult))
                link(dve.tensor_scalar(lam_t[:, 0, :], lam, -1.0, 0.0, ALU.mult, ALU.max))
                link(dve.scalar_tensor_tensor(lam_t[:, 3, :], lam_t[:, 3, :], 2.0, lam_t[:, 0, :], ALU.mult, ALU.add))
                dve.tensor_scalar(lam_t[:, 4, :], lam_t[:, 3, :], 2.0, None, ALU.mult)
                dve.tensor_scalar(lam_t[:, 5, :], lam_t[:, 3, :], -4.0, None, ALU.mult)
                dve.tensor_scalar(half_b[:, 0, :], par[:, C_BR:C_BR + DEPTH * 2 * LT], 0.5, None, ALU.mult)
                dve.tensor_scalar(half_b[:, 1, :], par[:, C_BI:C_BI + DEPTH * 2 * LT], 0.5, None, ALU.mult).then_inc(lam_ready, 1)

            dve.memset(mhalf[:], -0.5).then_inc(hid_ready, HID0)
            dve.memset(bn2[:], 0.0).then_inc(res_ready, HID0)
            dve.memset(bn6[:], 0.0).then_inc(hid_lo_ready, HID_LO0)
            dve.memset(ada_acc[:, 0, 0:1], 0.0).then_inc(acc_read, ACC0)
            dve.wait_ge(acc_read, ACC0)
            dve.wait_ge(par_in, 16)
            softplus()
            norm(0)
            for l in range(DEPTH):
                up_stage(l, 0)
                down_stage(l, 0)
                norm(3 * l + 1)
                in_stage(l)
                out_stage(l)
                norm(3 * l + 2)
                up_stage(l, 1)
                down_stage(l, 1)
                norm(3 * l + 3)

        @block.gpsimd
        def _(pool):
            chain = [0]

            def link(ins):
                chain[0] += 1
                ins.then_inc(pool_chain, 1)
                pool.wait_ge(pool_chain, chain[0])

            def bias_of(l, m):
                c = C_BADA + (l * NMOD + m) * KD
                return par[:, c:c + KD].unsqueeze(2).to_broadcast([P, KD, 2])

            def prep_norm(l, i):
                n = 3 * l + i
                at = [ADA_ORDER.index((l, 3 * i + j)) for j in range(2)]
                pool.wait_ge(mods_ready, MODS0 + max(at) + 1)
                a, b = at[0] * KD, at[1] * KD
                pool.tensor_tensor(n_shift[:, n, :, :], mods[:, a:a + KD, :], bias_of(l, 3 * i), ALU.add)
                link(pool.tensor_tensor(n_gain[:, n, :, :], mods[:, b:b + KD, :], bias_of(l, 3 * i + 1), ALU.add))
                link(pool.tensor_scalar(n_gain[:, n, :, :], n_gain[:, n, :, :], 1.0, None, ALU.add))
                g = C_GAIN + n * KD
                pool.tensor_tensor(n_gain[:, n, :, :], n_gain[:, n, :, :],
                                   par[:, g:g + KD].unsqueeze(2).to_broadcast([P, KD, 2]), ALU.mult).then_inc(prepped, 1)

            def prep_gate(l, i):
                n = 3 * l + i
                at = ADA_ORDER.index((l, 3 * i + 2))
                pool.wait_ge(mods_ready, MODS0 + at + 1)
                a = at * KD
                link(pool.tensor_tensor(gates[:, n, :, :], mods[:, a:a + KD, :], bias_of(l, 3 * i + 2), ALU.add))
                pool.tensor_scalar(gates[:, n, :, :], gates[:, n, :, :], 1.0 if i == 1 else 0.5, None,
                                   ALU.mult).then_inc(prepped, 1)

            def norm(n):
                w = dft(n)
                m4 = w // P
                for d in range(1, 7 if n else 1):
                    pool.wait_ge(sq_ready, KD * n + d + 1)
                    if d > 1:
                        pool.wait_ge(sqsum_ready, 6 * (n - 1) + d - 1)
                    pool.tensor_tensor(scr[:, 2, 0:w], scr[:, 2, 0:w], scr[:, d % 2, 0:w], ALU.add).then_inc(sqsum_ready, 1)
                pool.wait_ge(var_ready, n + 1)
                pool.tensor_tensor(tokr[:, 0:m4], tok[:, 0:m4], mhalf[:, 0:m4], ALU.pow).then_inc(rstd_ready, 1)
                if n in (0, 3 * DEPTH):
                    return
                if n:
                    pool.wait_ge(pre_done, n)
                for k in range(1, KD, 2):
                    pool.wait_ge(z_full_ready, KD // 2 * (n - 1) + k // 2 + 1)
                    pool.tensor_tensor(z_lo[:, k, 0:w], scr[:, k % 3, 0:w], z_hi[:, k, 0:w].bitcast(F32),
                                       ALU.subtract).then_inc(z_ready[1], 1)

            def in_stage(l):
                wl = SEQ if l == DEPTH - 1 else T
                for u in range(8):
                    r = u % 4
                    pool.wait_ge(ti_ready, 8 * l + u + 1)
                    pool.wait_ge(xc_ready, 4 * l + u // 2 + 1)
                    link(pool.tensor_tensor(l_bx[:, r, :], l_bx[:, r, :], xc[:, u // 2, :], ALU.mult))
                    pool.tensor_tensor(l_bx[:, r, :], l_bx[:, r, :], xc[:, u // 2, :], ALU.add).then_inc(bx_ready, 1)
                    if u == 3:
                        pool.wait_ge(vvar_ready, l + 1)
                        m4 = wl // P
                        link(pool.tensor_scalar(tok[:, 0:m4], bn2[:, 0:m4, 1], EPS, None, ALU.add))
                        pool.tensor_tensor(tokr[:, 0:m4], tok[:, 0:m4], mhalf[:, 0:m4], ALU.pow).then_inc(vrstd_ready, 1)
                for n_ in range(Y_POOL):
                    k = Y_ORDER[n_]
                    pool.wait_ge(y_hi_ready, 8 * l + n_ + 1)
                    src = y_lru if k < 4 else y_sgu
                    pool.tensor_tensor(y_lo[:, k, 0:wl], src[:, k % 4, 0:wl], y_hi[:, k, 0:wl].bitcast(F32),
                                       ALU.subtract).then_inc(y_lo_pool, 1)

            def zero_blocks(l):
                pool.wait_ge(slot_done, AT[l, "in"]["slot"])
                pool.memset(xpad[:], 0.0)
                pool.memset(bd[:], 0.0).then_inc(bd_zero, 1)

            pool.memset(c_cols[:], 0.0)
            pool.memset(ones[:], 1.0)
            pool.memset(sel[:], 0.0)
            link(pool.memset(ident[:], 0.0))
            for s in range(2):
                pool.memset(sel[:, s, s:s + 1], 1.0)
            pool.affine_select(out=ident[:], in_=ident[:], compare_op=ALU.not_equal, fill=1.0, base=0,
                               pattern=[[-1, P]], channel_multiplier=1).then_inc(const_ready, 1)
            pool.wait_ge(par_in, 16)
            norm(0)
            for l in range(DEPTH):
                prep_gate(l, 0)
                prep_norm(l, 1)
                norm(3 * l + 1)
                zero_blocks(l)
                prep_gate(l, 1)
                prep_norm(l, 2)
                in_stage(l)
                norm(3 * l + 2)
                prep_gate(l, 2)
                if l == 0:
                    prep_norm(1, 0)
                norm(3 * l + 3)


def _weight_stream(w_in, w_out, w_in_mix, w_out_mix):
    parts = []

    def columns(w):
        n = w.shape[1] // P
        return w.reshape(KD, P, n, P).transpose(2, 1, 0, 3).reshape(n, P, SLOT)

    for f in range(2):
        up = w_in[f].reshape(KD, P, 2, KF, P).transpose(3, 2, 1, 0, 4).reshape(UP_SLOTS, P, SLOT)
        down = np.zeros((KD, P, 24, P), w_out[f].dtype)
        down[:, :, :KF] = w_out[f].reshape(KF, P, KD, P).transpose(2, 1, 0, 3)
        down = down.reshape(KD, P, 3, SLOT).transpose(0, 2, 1, 3).reshape(DOWN_SLOTS, P, SLOT)
        parts += [up, down]
        if f == 0:
            w = LT * P
            v = w_in_mix[:, 3 * w:].reshape(4, 2, P, w).transpose(0, 2, 1, 3).reshape(4, P, SLOT)
            parts += [columns(w_in_mix[:, :w]), v, columns(w_in_mix[:, w:2 * w]),
                      columns(w_in_mix[:, 2 * w:3 * w]), columns(w_out_mix)]
    return parts


def _columns(a):
    a = np.asarray(a)
    return a.reshape(-1, P).T


def kernel(**inputs):
    import concourse.bacc as bacc
    from concourse.bass_utils import run_bass_kernel_spmd

    t = {k: np.asarray(v) for k, v in inputs.items()}
    x_t = np.concatenate([t["x"][0], t["ctx"][0]], axis=0).T.reshape(KD, P, T).transpose(1, 0, 2)
    cvec = np.stack([t["c"][0].reshape(KD, P), t["c_ctx"].reshape(KD, P)], axis=1)
    gains = np.stack([t["ffn1_norm_g"], t["mix_norm_g"], t["ffn2_norm_g"]], axis=1)
    conv = np.concatenate([t["lru_conv_w"], t["lru_conv_b"][:, None]], axis=1)
    params = np.concatenate([_columns(a) for a in (
        cvec, t["b_ada"], gains, t["final_norm_g"], conv, t["lru_b_r"], t["lru_b_i"], t["lru_lambda"],
        t["sgu_norm_g"])], axis=1)
    assert params.shape == (P, N_PAR)
    head_w = t["w_ada"][0, :, :2 * D].reshape(KD, P, 2, KD, P).transpose(3, 1, 0, 2, 4).reshape(KD, P, KD * 2 * P)
    ada_w = np.stack([t["w_ada"][l, :, m * D:(m + 1) * D] for l, m in ADA_ORDER])
    weights = np.concatenate([part for l in range(DEPTH) for part in _weight_stream(
        (t["ffn1_w_in"][l], t["ffn2_w_in"][l]), (t["ffn1_w_out"][l], t["ffn2_w_out"][l]),
        t["w_in_mix"][l], t["w_out_mix"][l])], axis=0)
    gate_w = np.stack([t["lru_w_r"], t["lru_w_i"]], axis=1).reshape(DEPTH, 2, 2, LT, 2, 64, 64)
    gate_w = gate_w.transpose(0, 4, 5, 1, 2, 3, 6).reshape(DEPTH, 2, 64, 16, 64)
    arrays = {
        "x_t": x_t, "params": params, "head_w": head_w, "ada_w": ada_w.reshape(len(ADA_ORDER) * KD, P, D), "weights": weights,
        "gate_w": gate_w, "sgu_w": t["sgu_w"].transpose(0, 3, 1, 2), "sgu_b": t["sgu_b"],
    }
    arrays = {k: np.ascontiguousarray(v) for k, v in arrays.items()}
    nc = bacc.Bacc("TRN2", target_bir_lowering=False, num_devices=1)
    args = [nc.dram_tensor(k, v.shape, F32, kind="ExternalInput").ap() for k, v in arrays.items()]
    out = nc.dram_tensor("out", (P, KD, SEQ), F32, kind="ExternalOutput").ap()
    build(nc, *args, out)
    got = run_bass_kernel_spmd(nc, [arrays], core_ids=[0]).results[0]["out"]
    return got.transpose(2, 1, 0).reshape(1, SEQ, D)
```
